# Optimizing a Trainium2 kernel written in Bass

```python
import math
import jax, jax.numpy as jnp
from jax import lax
import numpy as np

D_MODEL = 1024
BATCH = 1
SEQ = 256
DEPTH = 2

PLE_DIM = 256
HEAD_DIM = 64
DIFF_HEADS = 4
DIFF_QK = 2 * HEAD_DIM
DIFF_V = 2 * HEAD_DIM
FOX_HEADS = 4
FOX_DIM = HEAD_DIM
RET_HEADS = 4
RET_DIM = HEAD_DIM
WA = DIFF_HEADS * DIFF_V
WB = FOX_HEADS * FOX_DIM
WC = RET_HEADS * RET_DIM
MIX_WIDTH = WA + WB + WC
IN_SIZES = (DIFF_HEADS * DIFF_QK, DIFF_HEADS * DIFF_QK, WA, WB, WB, WB, FOX_HEADS, WC, WC, WC, WC)
IN_COLS = sum(IN_SIZES)
Q_BLOCK = 128
RET_CHUNK = 128
RET_THETA = 10000.0
D_FF_DENSE = 2816
N_EXPERTS = 8
TOP_K = 2
D_FF_EXPERT = 3584
N_DENSE = (DEPTH + 1) // 2
N_MOE = DEPTH // 2
EPS = 1e-6
NEG_INF = -1e30


def rmsnorm(x, g):
    xf = x.astype(jnp.float32)
    y = xf * lax.rsqrt(jnp.mean(xf * xf, axis=-1, keepdims=True) + EPS)
    return (y * g.astype(jnp.float32)).astype(x.dtype)

def head_groupnorm(x):
    xf = x.astype(jnp.float32)
    mu = jnp.mean(xf, axis=-1, keepdims=True)
    var = jnp.mean(jnp.square(xf - mu), axis=-1, keepdims=True)
    return ((xf - mu) * lax.rsqrt(var + EPS)).astype(x.dtype)

def split_heads(t, n_heads):
    B, S, _ = t.shape
    return t.reshape(B, S, n_heads, -1).transpose(0, 2, 1, 3)

def merge_heads(t):
    B, H, S, D = t.shape
    return t.transpose(0, 2, 1, 3).reshape(B, S, H * D)

def rotary(x):
    S, D = x.shape[2], x.shape[3]
    half = D // 2
    inv = RET_THETA ** (-jnp.arange(half, dtype=jnp.float32) / half)
    ang = jnp.arange(S, dtype=jnp.float32)[:, None] * inv[None, :]
    cos, sin = jnp.cos(ang).astype(x.dtype), jnp.sin(ang).astype(x.dtype)
    x1, x2 = x[..., :half], x[..., half:]
    return jnp.concatenate([x1 * cos - x2 * sin, x1 * sin + x2 * cos], axis=-1)

def causal_block_attention(q, k, v, scale, cum_logf=None):
    B, H, S, Dk = q.shape
    nb = S // Q_BLOCK
    q_blocks = q.reshape(B, H, nb, Q_BLOCK, Dk).transpose(2, 0, 1, 3, 4)
    k_pos = jnp.arange(S)
    xs = [jnp.arange(nb), q_blocks]
    if cum_logf is not None:
        xs.append(cum_logf.reshape(B, H, nb, Q_BLOCK).transpose(2, 0, 1, 3))

    def one_block(blk):
        i, q_i = blk[0], blk[1]
        s = jnp.einsum('bhqd,bhkd->bhqk', q_i, k).astype(jnp.float32) * scale
        if cum_logf is not None:
            s = s + blk[2][..., :, None] - cum_logf[:, :, None, :]
        q_pos = i * Q_BLOCK + jnp.arange(Q_BLOCK)
        s = jnp.where(k_pos[None, :] <= q_pos[:, None], s, NEG_INF)
        w = jax.nn.softmax(s, axis=-1).astype(v.dtype)
        return jnp.einsum('bhqk,bhkv->bhqv', w, v)

    o = lax.map(one_block, tuple(xs))
    return o.transpose(1, 2, 0, 3, 4).reshape(B, H, S, v.shape[-1])

def retention_chunkwise(q, k, v):
    B, H, S, Dk = q.shape
    Dv = v.shape[-1]
    nc = S // RET_CHUNK
    log_g = jnp.log1p(-jnp.exp2(-5.0 - jnp.arange(H, dtype=jnp.float32)))
    j = jnp.arange(RET_CHUNK, dtype=jnp.float32)
    diff = j[:, None] - j[None, :]
    inner = jnp.exp(jnp.where(diff[None] >= 0, diff[None] * log_g[:, None, None], -jnp.inf))
    q_dec = jnp.exp((j + 1.0)[None, :] * log_g[:, None])
    k_dec = jnp.exp((RET_CHUNK - 1.0 - j)[None, :] * log_g[:, None])
    c_dec = jnp.exp(RET_CHUNK * log_g)

    def to_chunks(t):
        return t.astype(jnp.float32).reshape(B, H, nc, RET_CHUNK, -1).transpose(2, 0, 1, 3, 4)

    def step(state, qkv):
        qc, kc, vc = qkv
        a = jnp.einsum('bhqd,bhkd->bhqk', qc, kc) * inner
        o = (jnp.einsum('bhqk,bhkv->bhqv', a, vc)
             + jnp.einsum('bhqd,bhdv->bhqv', qc * q_dec[:, :, None], state))
        state = state * c_dec[:, None, None] + jnp.einsum('bhkd,bhkv->bhdv', kc * k_dec[:, :, None], vc)
        return state, o

    state0 = jnp.zeros((B, H, Dk, Dv), jnp.float32)
    _, o = lax.scan(step, state0, (to_chunks(q), to_chunks(k), to_chunks(v)))
    return o.transpose(1, 2, 0, 3, 4).reshape(B, H, S, Dv).astype(v.dtype)

def hybrid_mixer(xn, w_in, b_forget, lq1, lk1, lq2, lk2, subln_g, ret_gn_g, w_out, layer_idx):
    B, S, _ = xn.shape
    proj = xn @ w_in
    qa, ka, va, qb, kb, vb, fb, qc, kc, vc, gc = jnp.split(proj, list(np.cumsum(IN_SIZES)[:-1]), axis=-1)

    qa = split_heads(qa, 2 * DIFF_HEADS)
    ka = split_heads(ka, 2 * DIFF_HEADS)
    va = jnp.repeat(split_heads(va, DIFF_HEADS), 2, axis=1)
    o = causal_block_attention(qa, ka, va, HEAD_DIM ** -0.5)
    o = o.reshape(B, DIFF_HEADS, 2, S, DIFF_V)
    lam_init = 0.8 - 0.6 * math.exp(-0.3 * layer_idx)
    lam = (jnp.exp(jnp.sum(lq1.astype(jnp.float32) * lk1.astype(jnp.float32)))
           - jnp.exp(jnp.sum(lq2.astype(jnp.float32) * lk2.astype(jnp.float32))) + lam_init)
    o_a = o[:, :, 0] - lam.astype(o.dtype) * o[:, :, 1]
    o_a = merge_heads(rmsnorm(o_a, subln_g) * (1.0 - lam_init))

    log_f = jax.nn.log_sigmoid((fb + b_forget).astype(jnp.float32))
    cum = jnp.cumsum(log_f, axis=1).transpose(0, 2, 1)
    o_b = causal_block_attention(split_heads(qb, FOX_HEADS), split_heads(kb, FOX_HEADS),
                                 split_heads(vb, FOX_HEADS), FOX_DIM ** -0.5, cum)
    o_b = merge_heads(o_b)

    qr = rotary(split_heads(qc, RET_HEADS))
    kr = rotary(split_heads(kc, RET_HEADS)) * (RET_DIM ** -0.5)
    o_c = retention_chunkwise(qr, kr, split_heads(vc, RET_HEADS))
    o_c = merge_heads(head_groupnorm(o_c)) * ret_gn_g
    o_c = jax.nn.silu(gc) * o_c

    return jnp.concatenate([o_a, o_b, o_c], axis=-1) @ w_out

def swiglu(x, wg, wu, wd):
    return (jax.nn.silu(x @ wg) * (x @ wu)) @ wd

def moe_swiglu(xn, router, wg, wu, wd):
    B, S, D = xn.shape
    t = xn.reshape(B * S, D)
    logits = (t @ router).astype(jnp.float32)
    top_val, top_idx = lax.top_k(logits, TOP_K)
    gates = jax.nn.softmax(top_val, axis=-1)
    combine = jnp.sum(jax.nn.one_hot(top_idx, N_EXPERTS, dtype=jnp.float32) * gates[..., None], axis=1)
    out = jnp.zeros_like(t)
    for e in range(N_EXPERTS):
        out = out + combine[:, e:e + 1].astype(t.dtype) * swiglu(t, wg[e], wu[e], wd[e])
    return out.reshape(B, S, D)

def first_inputs(seed: int = 0) -> dict:
    key = jax.random.key(seed)
    ks = jax.random.split(key, 26)
    f32 = jnp.float32

    def nrm(k, shape, scale):
        return jax.random.normal(k, shape, f32) * scale

    def gain(k, shape):
        return 1.0 + 0.05 * jax.random.normal(k, shape, f32)

    return {
        "x": nrm(ks[0], (BATCH, SEQ, D_MODEL), 1.0),
        "p": nrm(ks[1], (DEPTH, BATCH, SEQ, PLE_DIM), 1.0),
        "norm_mix": gain(ks[2], (DEPTH, D_MODEL)),
        "w_in": nrm(ks[3], (DEPTH, D_MODEL, IN_COLS), D_MODEL ** -0.5),
        "b_forget": 3.0 + 0.5 * jax.random.normal(ks[4], (DEPTH, FOX_HEADS), f32),
        "lambda_q1": nrm(ks[5], (DEPTH, HEAD_DIM), 0.1),
        "lambda_k1": nrm(ks[6], (DEPTH, HEAD_DIM), 0.1),
        "lambda_q2": nrm(ks[7], (DEPTH, HEAD_DIM), 0.1),
        "lambda_k2": nrm(ks[8], (DEPTH, HEAD_DIM), 0.1),
        "diff_subln": gain(ks[9], (DEPTH, DIFF_V)),
        "ret_gn": gain(ks[10], (DEPTH, WC)),
        "w_out": nrm(ks[11], (DEPTH, MIX_WIDTH, D_MODEL), MIX_WIDTH ** -0.5),
        "norm_ffn": gain(ks[12], (DEPTH, D_MODEL)),
        "dense_w_gate": nrm(ks[13], (N_DENSE, D_MODEL, D_FF_DENSE), D_MODEL ** -0.5),
        "dense_w_up": nrm(ks[14], (N_DENSE, D_MODEL, D_FF_DENSE), D_MODEL ** -0.5),
        "dense_w_down": nrm(ks[15], (N_DENSE, D_FF_DENSE, D_MODEL), D_FF_DENSE ** -0.5),
        "router": nrm(ks[16], (N_MOE, D_MODEL, N_EXPERTS), D_MODEL ** -0.5),
        "moe_w_gate": nrm(ks[17], (N_MOE, N_EXPERTS, D_MODEL, D_FF_EXPERT), D_MODEL ** -0.5),
        "moe_w_up": nrm(ks[18], (N_MOE, N_EXPERTS, D_MODEL, D_FF_EXPERT), D_MODEL ** -0.5),
        "moe_w_down": nrm(ks[19], (N_MOE, N_EXPERTS, D_FF_EXPERT, D_MODEL), D_FF_EXPERT ** -0.5),
        "ple_norm": gain(ks[20], (DEPTH, D_MODEL)),
        "ple_gate": nrm(ks[21], (DEPTH, D_MODEL, D_MODEL), D_MODEL ** -0.5),
        "ple_proj": nrm(ks[22], (DEPTH, PLE_DIM, D_MODEL), PLE_DIM ** -0.5),
        "final_norm": gain(ks[23], (D_MODEL,)),
    }

def first_block(x, p, norm_mix, w_in, b_forget, lambda_q1, lambda_k1, lambda_q2, lambda_k2,
              diff_subln, ret_gn, w_out, norm_ffn, dense_w_gate, dense_w_up, dense_w_down,
              router, moe_w_gate, moe_w_up, moe_w_down, ple_norm, ple_gate, ple_proj, final_norm):
    h = x
    for i in range(DEPTH):
        xn = rmsnorm(h, norm_mix[i])
        h = h + hybrid_mixer(xn, w_in[i], b_forget[i], lambda_q1[i], lambda_k1[i], lambda_q2[i],
                             lambda_k2[i], diff_subln[i], ret_gn[i], w_out[i], i)
        xn = rmsnorm(h, norm_ffn[i])
        j = i // 2
        if i % 2 == 0:
            h = h + swiglu(xn, dense_w_gate[j], dense_w_up[j], dense_w_down[j])
        else:
            h = h + moe_swiglu(xn, router[j], moe_w_gate[j], moe_w_up[j], moe_w_down[j])
        gate = jax.nn.sigmoid(rmsnorm(h, ple_norm[i]) @ ple_gate[i])
        h = h + gate * (p[i] @ ple_proj[i])
    return rmsnorm(h, final_norm)


MEM_LEN = 256
GROUP_WIDTH = D_MODEL // 2
D_MIX = 3 * GROUP_WIDTH
MOBA_HEAD_DIM = 64
MOBA_HEADS = GROUP_WIDTH // MOBA_HEAD_DIM
MOBA_BLOCK = 256
MOBA_TOPK = 3
MOBA_Q_CHUNK = 16
HGRN_HEAD_DIM = 128
HGRN_HEADS = GROUP_WIDTH // HGRN_HEAD_DIM
HGRN_CHUNK = 64
MEM_HEAD_DIM = 128
MEM_HEADS = GROUP_WIDTH // MEM_HEAD_DIM
ROPE_THETA = 500000.0
ROPE_DIM = MOBA_HEAD_DIM // 4
NORM_EPS = 1e-6
IN_COLS_2 = 3 * GROUP_WIDTH + 3 * GROUP_WIDTH + GROUP_WIDTH + D_MIX


def rms_norm(x, g):
    xf = x.astype(jnp.float32)
    y = xf * lax.rsqrt(jnp.mean(xf * xf, axis=-1, keepdims=True) + NORM_EPS)
    return (y * g.astype(jnp.float32)).astype(x.dtype)

def partial_rope(x, positions):
    half = ROPE_DIM // 2
    inv_freq = ROPE_THETA ** (-jnp.arange(half, dtype=jnp.float32) / half)
    ang = positions.astype(jnp.float32)[..., None] * inv_freq
    cos = jnp.cos(ang)[:, :, None, :]
    sin = jnp.sin(ang)[:, :, None, :]
    xr = x[..., :ROPE_DIM].astype(jnp.float32)
    x1, x2 = xr[..., :half], xr[..., half:]
    rot = jnp.concatenate([x1 * cos - x2 * sin, x2 * cos + x1 * sin], axis=-1).astype(x.dtype)
    return jnp.concatenate([rot, x[..., ROPE_DIM:]], axis=-1)

def moba_attention(q, k, v):
    B, S, H, D = q.shape
    BLK, QC = MOBA_BLOCK, MOBA_Q_CHUNK
    nb = -(-S // BLK)
    pad = nb * BLK - S
    topk = min(MOBA_TOPK, nb)
    kbh = jnp.pad(k, ((0, 0), (0, pad), (0, 0), (0, 0))).reshape(B, nb, BLK, H, D).transpose(0, 3, 1, 2, 4)
    vbh = jnp.pad(v, ((0, 0), (0, pad), (0, 0), (0, 0))).reshape(B, nb, BLK, H, D).transpose(0, 3, 1, 2, 4)
    kmean = jnp.mean(kbh.astype(jnp.float32), axis=3)
    scale = D ** -0.5
    nqc = S // QC
    qch = q.reshape(B, nqc, QC, H, D).transpose(1, 0, 3, 2, 4)
    bi = jnp.arange(B)[:, None, None, None]
    hi = jnp.arange(H)[None, :, None, None]
    blk_ids = jnp.arange(nb)

    def one_chunk(args):
        ci, qi = args
        start = ci * QC
        own = start // BLK
        qpos = start + jnp.arange(QC)
        gate = jnp.einsum('bhqd,bhnd->bhqn', qi.astype(jnp.float32), kmean)
        gate = jnp.where(blk_ids < own, gate, -jnp.inf)
        _, sel = lax.top_k(gate, topk)
        sel_ok = sel < own
        k_sel = kbh[bi, hi, sel]
        v_sel = vbh[bi, hi, sel]
        s_sel = jnp.einsum('bhqd,bhqkld->bhqkl', qi, k_sel).astype(jnp.float32) * scale
        s_sel = jnp.where(sel_ok[..., None], s_sel, -jnp.inf).reshape(B, H, QC, topk * BLK)
        k_own = lax.dynamic_index_in_dim(kbh, own, axis=2, keepdims=False)
        v_own = lax.dynamic_index_in_dim(vbh, own, axis=2, keepdims=False)
        kpos = own * BLK + jnp.arange(BLK)
        s_own = jnp.einsum('bhqd,bhld->bhql', qi, k_own).astype(jnp.float32) * scale
        s_own = jnp.where(kpos[None, :] <= qpos[:, None], s_own, -jnp.inf)
        p = jax.nn.softmax(jnp.concatenate([s_sel, s_own], axis=-1), axis=-1).astype(v.dtype)
        p_sel = p[..., :topk * BLK].reshape(B, H, QC, topk, BLK)
        p_own = p[..., topk * BLK:]
        return (jnp.einsum('bhqkl,bhqkld->bhqd', p_sel, v_sel)
                + jnp.einsum('bhql,bhld->bhqd', p_own, v_own))

    o = lax.map(one_chunk, (jnp.arange(nqc), qch))
    return o.transpose(1, 0, 3, 2, 4).reshape(B, S, H, D)

def hgrn2_chunkwise(q, f_logit, i, lb):
    B, S, H, DK = q.shape
    DV = i.shape[-1]
    C = HGRN_CHUNK
    NC = S // C
    fl = f_logit.astype(jnp.float32)
    qf = jax.nn.silu(q.astype(jnp.float32))
    log_f = jnp.logaddexp(jnp.log(lb), jnp.log1p(-lb) + jax.nn.log_sigmoid(fl))
    kf = (1.0 - lb) * jax.nn.sigmoid(-fl)
    vf = i.astype(jnp.float32)

    def to_chunks(t):
        return t.reshape(B, NC, C, H, t.shape[-1]).transpose(1, 0, 3, 2, 4)

    causal = jnp.tril(jnp.ones((C, C), dtype=bool))

    def step(state, inp):
        qc, lfc, kc, vc = inp
        A = jnp.cumsum(lfc, axis=2)
        diff = A[:, :, :, None, :] - A[:, :, None, :, :]
        decay = jnp.exp(jnp.where(causal[:, :, None], diff, -jnp.inf))
        scores = jnp.einsum('bhtd,bhtsd,bhsd->bhts', qc, decay, kc)
        o = (jnp.einsum('bhts,bhsv->bhtv', scores, vc)
             + jnp.einsum('bhtd,bhdv->bhtv', qc * jnp.exp(A), state))
        A_end = A[:, :, -1:, :]
        state = (jnp.exp(A_end[:, :, 0, :])[..., None] * state
                 + jnp.einsum('bhsd,bhsv->bhdv', kc * jnp.exp(A_end - A), vc))
        return state, o

    s0 = jnp.zeros((B, H, DK, DV), jnp.float32)
    _, o = lax.scan(step, s0, (to_chunks(qf), to_chunks(log_f), to_chunks(kf), to_chunks(vf)))
    return o.transpose(1, 0, 3, 2, 4).reshape(B, S, H, DV)

def memory_attention(q, k, v):
    scale = q.shape[-1] ** -0.5
    s = jnp.einsum('bshd,bmhd->bhsm', q, k).astype(jnp.float32) * scale
    p = jax.nn.softmax(s, axis=-1).astype(v.dtype)
    return jnp.einsum('bhsm,bmhd->bshd', p, v)

def second_inputs(seed: int = 0) -> dict:
    key = jax.random.key(seed)
    ks = jax.random.split(key, 14)
    f32 = jnp.float32

    def gain(k, shape):
        return 1.0 + 0.02 * jax.random.normal(k, shape, f32)

    return {
        "x": jax.random.normal(ks[0], (BATCH, SEQ, D_MODEL), f32),
        "mem": jax.random.normal(ks[1], (BATCH, MEM_LEN, D_MODEL), f32),
        "positions": jnp.tile(jnp.arange(SEQ, dtype=jnp.int32)[None, :], (BATCH, 1)),
        "norm_g": gain(ks[2], (DEPTH, D_MODEL)),
        "w_in": jax.random.normal(ks[3], (DEPTH, D_MODEL, IN_COLS_2), f32) * D_MODEL ** -0.5,
        "w_out": jax.random.normal(ks[4], (DEPTH, D_MIX, D_MODEL), f32) * D_MIX ** -0.5,
        "moba_q_norm": gain(ks[5], (DEPTH, MOBA_HEAD_DIM)),
        "moba_k_norm": gain(ks[6], (DEPTH, MOBA_HEAD_DIM)),
        "hgrn_lb_logits": 0.5 * jax.random.normal(ks[7], (DEPTH, GROUP_WIDTH), f32),
        "hgrn_o_norm": gain(ks[8], (DEPTH, HGRN_HEAD_DIM)),
        "mem_norm_g": gain(ks[9], (DEPTH, D_MODEL)),
        "w_mem_kv": jax.random.normal(ks[10], (DEPTH, D_MODEL, 2 * GROUP_WIDTH), f32) * D_MODEL ** -0.5,
        "mem_q_norm": gain(ks[11], (DEPTH, MEM_HEAD_DIM)),
        "mem_k_norm": gain(ks[12], (DEPTH, MEM_HEAD_DIM)),
    }

def second_block(x, mem, positions, norm_g, w_in, w_out, moba_q_norm, moba_k_norm, hgrn_lb_logits,
              hgrn_o_norm, mem_norm_g, w_mem_kv, mem_q_norm, mem_k_norm):
    B, S, _ = x.shape
    M = mem.shape[1]
    G = GROUP_WIDTH
    lb_all = jnp.cumsum(jax.nn.softmax(hgrn_lb_logits.astype(jnp.float32), axis=0), axis=0)
    lb_all = lb_all - lb_all[0:1]
    split_points = [G * n for n in range(1, 8)]
    for l in range(DEPTH):
        h = rms_norm(x, norm_g[l])
        proj = h @ w_in[l]
        q_a, k_a, v_a, q_h, f_h, i_h, q_m, z = jnp.split(proj, split_points, axis=-1)

        qa = partial_rope(rms_norm(q_a.reshape(B, S, MOBA_HEADS, MOBA_HEAD_DIM), moba_q_norm[l]), positions)
        ka = partial_rope(rms_norm(k_a.reshape(B, S, MOBA_HEADS, MOBA_HEAD_DIM), moba_k_norm[l]), positions)
        va = v_a.reshape(B, S, MOBA_HEADS, MOBA_HEAD_DIM)
        o_a = moba_attention(qa, ka, va).reshape(B, S, G)

        o_h = hgrn2_chunkwise(q_h.reshape(B, S, HGRN_HEADS, HGRN_HEAD_DIM),
                              f_h.reshape(B, S, HGRN_HEADS, HGRN_HEAD_DIM),
                              i_h.reshape(B, S, HGRN_HEADS, HGRN_HEAD_DIM),
                              lb_all[l].reshape(HGRN_HEADS, HGRN_HEAD_DIM))
        o_h = rms_norm(o_h, hgrn_o_norm[l]).astype(x.dtype).reshape(B, S, G)

        kv_m = rms_norm(mem, mem_norm_g[l]) @ w_mem_kv[l]
        k_m, v_m = jnp.split(kv_m, 2, axis=-1)
        km = rms_norm(k_m.reshape(B, M, MEM_HEADS, MEM_HEAD_DIM), mem_k_norm[l])
        vm = v_m.reshape(B, M, MEM_HEADS, MEM_HEAD_DIM)
        qm = rms_norm(q_m.reshape(B, S, MEM_HEADS, MEM_HEAD_DIM), mem_q_norm[l])
        o_m = memory_attention(qm, km, vm).reshape(B, S, G)

        y = jnp.concatenate([o_a, o_h, o_m], axis=-1) * jax.nn.silu(z)
        x = x + y @ w_out[l]
    return x


def setup_inputs(seed=0):
    out = dict(first_inputs(seed))
    for name, value in second_inputs(seed + 1).items():
        if name != "x":
            out[name + "_2"] = value
    return out


def reference(
    x, p, norm_mix, w_in, b_forget, lambda_q1, lambda_k1, lambda_q2, lambda_k2, diff_subln,
    ret_gn, w_out, norm_ffn, dense_w_gate, dense_w_up, dense_w_down, router, moe_w_gate,
    moe_w_up, moe_w_down, ple_norm, ple_gate, ple_proj, final_norm, mem_2, positions_2,
    norm_g_2, w_in_2, w_out_2, moba_q_norm_2, moba_k_norm_2, hgrn_lb_logits_2, hgrn_o_norm_2,
    mem_norm_g_2, w_mem_kv_2, mem_q_norm_2, mem_k_norm_2,
):
    x = first_block(
        x, p, norm_mix, w_in, b_forget, lambda_q1, lambda_k1, lambda_q2, lambda_k2, diff_subln,
        ret_gn, w_out, norm_ffn, dense_w_gate, dense_w_up, dense_w_down, router, moe_w_gate,
        moe_w_up, moe_w_down, ple_norm, ple_gate, ple_proj, final_norm,
    )
    return second_block(
        x, mem_2, positions_2, norm_g_2, w_in_2, w_out_2, moba_q_norm_2, moba_k_norm_2,
        hgrn_lb_logits_2, hgrn_o_norm_2, mem_norm_g_2, w_mem_kv_2, mem_q_norm_2, mem_k_norm_2,
    )


_drawn_inputs = setup_inputs


def setup_inputs(seed=0):
    import zlib

    import numpy as np

    out = dict(_drawn_inputs(seed))
    spreads = {}
    factors = {'ple_norm': 3.995,
     'norm_g_2': 4.072,
     'moba_q_norm_2': 8.0,
     'moba_k_norm_2': 8.0,
     'hgrn_lb_logits_2': 3.449,
     'hgrn_o_norm_2': 6.394,
     'mem_norm_g_2': 8.0,
     'mem_q_norm_2': 8.0,
     'mem_k_norm_2': 8.0}
    for name, (base, spread) in spreads.items():
        noise = np.random.default_rng([zlib.crc32(name.encode()), seed]).standard_normal(out[name].shape)
        drawn = base * np.exp(spread * noise) if base else spread * noise
        out[name] = __import__('jax').numpy.asarray(drawn.astype(out[name].dtype))
    for name, factor in factors.items():
        out[name] = (out[name] * factor).astype(out[name].dtype)
    return out
```

```python
import math
from contextlib import ExitStack

import numpy as np

import concourse.bass as bass
from concourse import mybir

F32 = mybir.dt.float32
I32 = mybir.dt.int32
U8 = mybir.dt.uint8
ALU = mybir.AluOpType
ACT = mybir.ActivationFunctionType
AX_X = mybir.AxisListType.X

P = 128
SEQ = 256
NT = SEQ // P
D = 1024
KB = D // P
LAYERS = 2
EPS = 1e-6
NEG = -1e30

DIFF_UNITS = 8
HEADS4 = 4
FF_DENSE = 2816
FB_DENSE = FF_DENSE // P
N_EXPERTS = 8
FF_EXPERT = 3584
CHUNK = 512
GROUPS = FF_EXPERT // CHUNK
G = 512
DMIX = 3 * G
KB2 = DMIX // P
MOBA_HEADS = 8
ROPE_HALF = 8
SLOTS = 7
SLOT = KB * CHUNK
LEVELS = 7

TWO_PI = 2.0 * math.pi
PI_HI = 6.28125
PI_MID = float(np.float32(TWO_PI - PI_HI))
PI_LO = float(TWO_PI - PI_HI - PI_MID)
ROUND = 12582912.0
AHEAD = 3


def lam_init(layer):
    return 0.8 - 0.6 * math.exp(-0.3 * layer)


def constants():
    t = np.arange(P)
    causal = np.where(t[None, :] <= t[:, None], 0.0, NEG).astype(np.float32)
    log_g = np.log1p(-np.exp2(-5.0 - np.arange(HEADS4)))
    diff = t[None, :] - t[:, None]
    decay = np.zeros((P, HEADS4, 3, P), np.float32)
    for h in range(HEADS4):
        same = np.where(diff >= 0, np.exp(np.maximum(diff, 0) * log_g[h]), 0.0)
        decay[:, h, 0] = decay[:, h, 2] = 0.125 * same
        decay[:, h, 1] = 0.125 * np.exp((diff + P) * log_g[h])
    inv = 10000.0 ** (-np.arange(32) / 32.0).astype(np.float32)
    ang = (np.arange(SEQ, dtype=np.float32)[:, None] * inv.astype(np.float32)[None, :]).astype(np.float32)
    rot = np.stack([np.cos(ang), np.sin(ang)]).astype(np.float32).reshape(2, NT, P, 32)
    rot = np.ascontiguousarray(rot.transpose(2, 0, 1, 3))
    masks = np.zeros((P, LEVELS + 1, P), np.float32)
    s, q = t[:, None], t[None, :]
    masks[:, 0] = s == q
    for lv in range(LEVELS):
        b = 1 << lv
        masks[:, lv + 1] = (s // (2 * b) == q // (2 * b)) & (s % (2 * b) < b) & (q % (2 * b) >= b)
    before = (s < q).astype(np.float32)
    slot = np.broadcast_to(t[None, :].astype(np.float32), (P, P))
    route = np.ascontiguousarray(np.stack([before, np.ones((P, P), np.float32), slot], 1))
    inv_rope = (500000.0 ** (-np.arange(ROPE_HALF, dtype=np.float32) / ROPE_HALF)).astype(np.float32)
    inv_rope = np.ascontiguousarray(np.broadcast_to(inv_rope, (P, ROPE_HALF)))
    return {"c_ident": np.eye(P, dtype=np.float32), "c_causal": causal, "c_decay": decay,
            "c_rot": rot, "c_masks": masks, "c_route": route, "c_inv_rope": inv_rope}


def program(nc, io, out, cut=99):
    ctx = ExitStack()
    with ctx:
        def sb(name, shape, dt=F32):
            return ctx.enter_context(nc.sbuf_tensor(name, shape, dt))

        def sem(name):
            return ctx.enter_context(nc.semaphore(name))

        ring = sb("ring", [P, SLOTS, SLOT])
        h = sb("h", [P, NT, D])
        yf = sb("yf", [P, NT * DMIX])
        xn = yf[:, 0:NT * D].rearrange("p (t d) -> p t d", t=NT)
        y1 = xn
        y2 = yf[:, :].rearrange("p (t d) -> p t d", t=NT)
        fox = yf[0:HEADS4, NT * D:NT * DMIX].rearrange("p (r s) -> p r s", r=4)
        xT = sb("xT", [P, KB2, SEQ])
        mem_src = xT[:, 0:KB, :].rearrange("p k s -> p (k s)").rearrange("p (t d) -> p t d", t=NT)
        a1 = sb("a1", [P, NT * G])
        a2 = sb("a2", [P, NT * G])
        qT = sb("qT", [P, 8, SEQ])
        kT = sb("kT", [P, 8, SEQ])
        v = sb("v", [P, NT, D])
        at = sb("at", [P, 12 * P])
        decay = at[:, :].rearrange("p (h m) -> p h m", h=HEADS4)
        atH = at[:, :].rearrange("p (b h t) -> p b h t", b=3, h=HEADS4)
        probs = sb("probs", [P, 2, 512])
        probsT = sb("probsT", [P, 2, 512])
        scr = sb("scr", [P, NT * G])
        sg = sb("sg", [P, NT, 256])
        ident = sb("ident", [P, P])
        causal = sb("causal", [P, P])
        masks = sb("masks", [P, LEVELS + 1, P], U8)
        rot = sb("rot", [P, 2, NT, 32])
        gcols = sb("gcols", [P, 10, KB])
        g_subln = sb("g_subln", [P, LAYERS, P])
        g_ret = sb("g_ret", [P, LAYERS, 256])
        g_moba = sb("g_moba", [P, 2, LAYERS, 64])
        g_hgrn = sb("g_hgrn", [P, LAYERS, P])
        g_mem = sb("g_mem", [P, 2, LAYERS, P])
        bforget = sb("bforget", [HEADS4, LAYERS])
        rope = sb("rope", [P, 2, NT, ROPE_HALF])
        inv_rope = sb("inv_rope", [P, ROPE_HALF])
        pos_i = sb("pos_i", [P, NT], I32)
        lbs = sb("lbs", [P, 2, LAYERS, HEADS4])
        lam = sb("lam", [P, LAYERS])
        stat = sb("stat", [P, 2, 16])
        ssum = sb("ssum", [P, NT])
        rowsum = sb("rowsum", [P, 8 * NT])
        negmax = sb("negmax", [P, 8 * NT])
        rinv = sb("rinv", [P, 8 * NT])
        routing = sb("routing", [P, 10, NT, N_EXPERTS])
        rtw = sb("rtw", [P, KB, N_EXPERTS])
        lone = sb("lone", [P, 8])
        marks = sb("marks", [P, 32])
        act_marks = sb("act_marks", [P, 4])
        flag_i = sb("flag_i", [1, 1], I32)
        bank = [ctx.enter_context(nc.psum_tensor(f"bank{i}", [P, 512], F32)) for i in range(8)]

        xg = qT[:, 0:4, :].rearrange("p a b -> p (a b)").rearrange("p (k s) -> p k s", k=KB)
        yx = qT[:, 4:8, :].rearrange("p a b -> p (a b)")
        hm = kT[:, 0:4, :].rearrange("p a b -> p (a b)").rearrange("p (r n) -> p r n", r=2)
        hT = kT[:, 4:8, :].rearrange("p a b -> p (a b)").rearrange("p (r f s) -> p r f s", r=2, f=4)
        gated = v[:, 0, :].rearrange("p (r n) -> p r n", r=2)
        pickP = v[:, 1, 0:256].rearrange("p (t s) -> p t s", t=NT)
        pickG = v[:, 1, 256:512].rearrange("p (t s) -> p t s", t=NT)
        pickGT = v[:, 1, 512:768]
        route = a1[:, 0:3 * P].rearrange("p (r s) -> p r s", r=3)
        hTd = kT
        g_final = a2[:, :]
        pin = a1[:, 512:1024].rearrange("p (t d) -> p t d", t=NT)
        pT = a1[:, 0:512].rearrange("p (k s) -> p k s", k=2)
        gatebuf = probs
        zbuf = probs

        landed = [sem(f"slot{i}_landed") for i in range(SLOTS)]
        rows_used = sem("row_chunks_used")
        consts_in, p_in, route_in, mem_in = sem("consts_in"), sem("p_in"), sem("route_in"), sem("mem_in")
        final_in, out_written = sem("final_in"), sem("out_written")
        unit_full, unit_act, unit_dve = sem("unit_full"), sem("unit_taken_act"), sem("unit_taken_dve")
        act_step, dve_step = sem("act_step"), sem("dve_step")
        dve_asks, act_answers = sem("dve_asks"), sem("act_answers")
        setup_dve, squares = sem("setup_dve"), sem("squares_summed")
        xn_ready, h_ready = sem("xn_ready"), sem("h_ready")
        att_scores, att_max, att_exp = sem("att_scores"), sem("att_max"), sem("att_exp")
        att_turned, att_copied, att_pv = sem("att_turned"), sem("att_copied"), sem("att_pv")
        cum_ready, rotated, normed = sem("cum_ready"), sem("rotated"), sem("heads_normed")
        ret_scores, ret_weights, ret_pv = sem("ret_scores"), sem("ret_weights"), sem("ret_pv")
        out_taken, y_ready, acc_full = sem("out_banks_taken"), sem("y_ready"), sem("acc_full")
        silu_done, hid_ready, z_used, gate_used = sem("silu_done"), sem("hidden_ready"), sem("z_used"), sem("gate_used")
        hg_qk, hg_scores, hg_pv = sem("hg_qk_ready"), sem("hg_scores"), sem("hg_pv")
        hg_placed = sem("hg_scores_placed")
        members_ready, rank_max, route_ready = sem("members_ready"), sem("rank_max_ready"), sem("route_ready")
        moe_names = ("sel", "tfull", "tact", "tdve", "gate", "up", "silu", "hm", "down", "y", "step")
        moe_sems = [{n: sem(f"moe{p}_{n}") for n in moe_names} for p in range(2)]
        ovf_landed = [sem(f"slot{i}_landed_overflow") for i in range(SLOTS)]

        chunks, where = [], {}
        units, unit_at = [], {}
        owner_count = {"act": 0, "dve": 0}

        slot_loads = [0] * SLOTS
        place_in_ring = [0]
        freed_by = {}
        row_chunks = [0]

        def chunk(key, src, kb, cols, by=None):
            slot = place_in_ring[0] % SLOTS
            place_in_ring[0] += 1
            slot_loads[slot] += 1
            where[key] = (slot, slot_loads[slot], kb, cols)
            if by is None:
                row_chunks[0] += 1
                by = ("rows", row_chunks[0])
            freed_by[key] = by
            chunks.append((key, src))

        def unit(key, owner):
            owner_count[owner] += 1
            unit_at[key] = (len(units), owner, owner_count[owner])
            units.append(key)

        def cols_of(w, c0, n):
            return w[:, c0:c0 + n].rearrange("(k p) n -> p k n", p=P)

        def rows_of(w, k0, nk):
            return w[k0 * P:(k0 + nk) * P, :].rearrange("(k p) n -> p k n", p=P)

        norm_no = {}

        def plan_norm(name):
            norm_no[name] = len(norm_no)
            for j in range(4):
                unit(("norm", name, j), "act" if j % 2 == 0 else "dve")

        MIX1 = (("qa", 0, 512, "act", "act"), ("ka", 512, 512, "dve", "dve"), ("va", 1024, 512, "act", "act"),
                ("qkb", 1536, 512, "act", "dve"), ("vfb", 2048, 260, "dve", "dve"),
                ("qkc", 2308, 512, "dve", "dve"), ("vgc", 2820, 512, "act", "act"))
        for l in range(LAYERS):
            plan_norm(("mix", l))
            for name, c0, w, own0, own1 in MIX1:
                chunk((name, l), cols_of(io["w_in"][l], c0, w), KB, w, ("unit", (name, l, 1)))
                unit((name, l, 0), own0)
                unit((name, l, 1), own1)
            unit(("qcT", l), "act")
            unit(("kcT", l), "act")
            for j in range(4):
                unit(("yT", l, j), "act" if j % 2 == 0 else "dve")
            for c in range(2):
                chunk(("wo", l, c), rows_of(io["w_out"][l], 4 * c, 4), 4, D, ("sum", ("wo", l)) if c == 1 else None)
            plan_norm(("ffn", l))
            if l == 0:
                wg, wu, wd = io["dense_w_gate"][0], io["dense_w_up"][0], io["dense_w_down"][0]
                for f in range(FB_DENSE):
                    if f % 4 == 0:
                        nb = min(4, FB_DENSE - f)
                        chunk(("dg", f // 4), cols_of(wg, f * P, nb * P), KB, nb * P, ("unit", ("ff", f + nb - 1)))
                        chunk(("du", f // 4), cols_of(wu, f * P, nb * P), KB, nb * P, ("unit", ("ff", f + nb - 1)))
                        chunk(("dd", f // 4), rows_of(wd, f, nb), nb, D,
                              ("sum", ("ffn", 0)) if f + nb == FB_DENSE else None)
                    unit(("ff", f), "dve")
            else:
                for name in ("logits", "rank", "rank_max"):
                    unit((name,), "dve")
                place_in_ring[0] += -place_in_ring[0] % SLOTS
                assert 3 * GROUPS % SLOTS == 0
                moe_base = list(slot_loads)
                chunks.append(("moe", None))
                for slot in range(SLOTS):
                    slot_loads[slot] += 3 * GROUPS // SLOTS * N_EXPERTS
            plan_norm(("ple", l))
            unit(("pT", l), "act")
            chunk(("pp", l), rows_of(io["ple_proj"][l], 0, 2), 2, D, ("unit", ("pproj", l, 1, 1)))
            for j in range(2):
                chunk(("pg", l, j), cols_of(io["ple_gate"][l], j * CHUNK, CHUNK), KB, CHUNK,
                      ("unit", ("gate", l, j, 1)))
                for i in range(NT):
                    unit(("gate", l, j, i), "act")
                    unit(("pproj", l, j, i), "dve")
        norm_no["final"] = len(norm_no)
        for l in range(LAYERS):
            w2, wm = io["w_in_2"][l], io["w_mem_kv_2"][l]
            plan_norm(("mem", l))
            for n, name in enumerate(("km", "vm")):
                chunk((name, l), cols_of(wm, n * G, G), KB, G, ("unit", (name, l, 1)))
                for i in range(NT):
                    unit((name, l, i), "dve" if name == "km" else "act")
            for j in range(2):
                unit(("kmT", l, j), "act")
            plan_norm(("mix2", l))
            for name, n in (("qm", 6), ("qa2", 0), ("ka2", 1), ("va2", 2)):
                chunk((name, l), cols_of(w2, n * G, G), KB, G, ("unit", (name, l, 1)))
                for i in range(NT):
                    unit((name, l, i), "act" if name == "va2" else "dve")
                if name == "qm":
                    for j in range(2):
                        unit(("qmT", l, j), "act")
            for name in ("qaT2", "kaT2"):
                for j in range(2):
                    unit((name, l, j), "act")
            for name, n in (("qh", 3), ("fh", 4), ("ih", 5)):
                chunk((name, l), cols_of(w2, n * G, G), KB, G, ("unit", (name, l, 1)))
                for i in range(2):
                    unit((name, l, i), "act")
            for c in range(3):
                chunk(("z", l, c), cols_of(w2, (7 + c) * G, G), KB, G, ("unit", ("z", l, c, 1)))
                for i in range(NT):
                    unit(("z", l, c, i), "act")
            for j in range(6):
                unit(("yT2", l, j), "act" if j % 2 == 0 else "dve")
            for c in range(3):
                chunk(("wo2", l, c), rows_of(io["w_out_2"][l], 4 * c, 4), 4, D, ("sum", ("wo2", l)) if c == 2 else None)

        att_first, att_n, out_use = {}, 0, {}
        for l in range(LAYERS):
            for name, n in (("diff", 8), ("fox", 4)):
                att_first[name, l], att_n = att_n, att_n + n
                out_use[name, l] = len(out_use)
            out_use["ret", l] = len(out_use)
            out_use["wo", l] = len(out_use)
            if l == 0:
                out_use["ffn", 0] = len(out_use)
        for l in range(LAYERS):
            for name, n in (("moba", 8), ("memory", 4)):
                att_first[name, l], att_n = att_n, att_n + n
                out_use[name, l] = len(out_use)
            out_use["hgrn", l] = len(out_use)
            out_use["wo2", l] = len(out_use)
        acc_no = {key: n for n, key in enumerate([("wo", 0), ("ffn", 0), ("wo", 1), ("wo2", 0), ("wo2", 1)])}
        h_at = {key: n + 1 for n, key in enumerate([("wo", 0), ("ffn", 0), ("ple", 0), ("wo", 1), ("ffn", 1),
                                                    ("ple", 1), "final", ("wo2", 0), ("wo2", 1)])}
        norm_src = {("ffn", 0): ("wo", 0), ("ple", 0): ("ffn", 0), ("mix", 1): ("ple", 0), ("ffn", 1): ("wo", 1),
                    ("ple", 1): ("ffn", 1), "final": ("ple", 1), ("mix2", 0): "final", ("mix2", 1): ("wo2", 0)}
        norm_gain = {("mix", 0): 0, ("mix", 1): 1, ("ffn", 0): 2, ("ffn", 1): 3, ("ple", 0): 4, ("ple", 1): 5,
                     ("mix2", 0): 6, ("mix2", 1): 7, ("mem", 0): 8, ("mem", 1): 9}

        def weights(key):
            slot, _, kb, cols = where[key]
            return ring[:, slot, 0:kb * cols].rearrange("p (k n) -> p k n", k=kb)

        def arrived(eng, key):
            slot, n, _, _ = where[key]
            eng.wait_ge(landed[slot], 16 * n)

        def bank_of(key):
            return bank[unit_at[key][0] % 4]

        def filled(eng, key):
            eng.wait_ge(unit_full, unit_at[key][0] + 1)

        def emptied(eng, key):
            _, owner, n = unit_at[key]
            eng.wait_ge(unit_act if owner == "act" else unit_dve, n)

        def free_bank(pe, key):
            n = unit_at[key][0]
            if n >= 4:
                emptied(pe, units[n - 4])

        def tok(i):
            return slice(i * P, (i + 1) * P)

        def halves(t, owner_rows=None):
            return [t[:, i, :] for i in range(NT)]

        def norm_input(eng, name):
            if name[0] == "mem":
                eng.wait_ge(mem_in, 16 * (name[1] + 1))
                return mem_src
            if name in norm_src:
                eng.wait_ge(h_ready, h_at[norm_src[name]])
            else:
                eng.wait_ge(consts_in, CONSTS)
            return h

        def att_shape(name):
            if name == "memory":
                return 4, 128, ((0, 256), (256, 256))
            return {"diff": 8, "fox": 4, "moba": 8}[name], 128 if name == "diff" else 64, ((0, 128), (128, 256))

        def att_operands(name, u):
            if name == "memory":
                return qT[:, 4 + u, :], kT[:, 4 + u, :], v[:, :, 512 + 128 * u:640 + 128 * u]
            blk = {"diff": 0, "fox": 4, "moba": 0}[name] + u // 2
            rows = slice(64 * (u % 2), 64 * (u % 2) + 64)
            val = {"diff": slice(128 * (u // 2), 128 * (u // 2) + 128), "fox": slice(512 + 64 * u, 576 + 64 * u),
                   "moba": slice(64 * u, 64 * u + 64)}[name]
            return qT[rows, blk, :], kT[rows, blk, :], v[:, :, val]

        def att_out(name, u, t):
            n, dv, _ = att_shape(name)
            col = (u * NT + t) * dv
            first = {"diff": 4, "fox": 4, "moba": 4, "memory": 6}[name]
            return bank[first + col // 512][:, col % 512:col % 512 + dv]

        def spread(vec, shape):
            return vec.partition_broadcast(P)

        loads = [(ident[:, :], io["c_ident"]), (causal[:, :], io["c_causal"]),
                 (decay, io["c_decay"].rearrange("p h b t -> p h (b t)")),
                 (rot[:, :, :, :], io["c_rot"]), (a2[:, :], io["c_masks"].rearrange("p n t -> p (n t)")),
                 (inv_rope[:, :], io["c_inv_rope"]),
                 (pos_i[:, :], io["l_positions"])]
        loads.append((gcols[:, :, :], io["l_gain_columns"]))
        loads.append((lbs[:, 0, :, :], io["l_bound_logits"]))
        loads.append((bforget[:, :], io["l_forget_bias"]))
        for l in range(LAYERS):
            loads.append((g_subln[:, l, :], io["diff_subln"][l].partition_broadcast(P)))
            loads.append((g_ret[:, l, :], io["ret_gn"][l].partition_broadcast(P)))
            loads.append((g_moba[:, 0, l, :], io["moba_q_norm_2"][l].partition_broadcast(P)))
            loads.append((g_moba[:, 1, l, :], io["moba_k_norm_2"][l].partition_broadcast(P)))
            loads.append((g_hgrn[:, l, :], io["hgrn_o_norm_2"][l].partition_broadcast(P)))
            loads.append((g_mem[:, 0, l, :], io["mem_q_norm_2"][l].partition_broadcast(P)))
            loads.append((g_mem[:, 1, l, :], io["mem_k_norm_2"][l].partition_broadcast(P)))
            for n, name in enumerate(("lambda_q1", "lambda_k1", "lambda_q2", "lambda_k2")):
                at0 = (n * LAYERS + l) * 64
                loads.append((scr[:, at0:at0 + 64], io[name][l].partition_broadcast(P)))
        loads.append((rtw[:, :, :], io["router"][0].rearrange("(k p) n -> p k n", p=P)))
        loads.append((h[:, :, :], io["x"][0].rearrange("(t p) d -> p t d", p=P)))
        CONSTS = 16 * len(loads)

        block = ctx.enter_context(nc.Block())

        @block.sync
        def _(sp):
            for dst, src in loads[-1:]:
                sp.dma_start(dst, src).then_inc(consts_in, 16)

            def before(key):
                if key[0] == "pp":
                    l = key[1]
                    filled(sp, ("norm", ("ple", l), 0))
                    sp.dma_start(pin, io["p"][l, 0].rearrange("(t p) d -> p t d", p=P)).then_inc(p_in, 16)
                if key == ("pg", 1, 0):
                    sp.dma_start(g_final, io["final_norm"].partition_broadcast(P)).then_inc(final_in, 16)
                if key[0] == "km":
                    l = key[1]
                    filled(sp, ("pproj", 1, 1, 1) if l == 0 else ("yT2", 0, 5))
                    if l == 1:
                        sp.wait_ge(acc_full, acc_no["wo2", 0] + 1)
                    sp.dma_start(mem_src, io["mem_2"][0].rearrange("(t p) d -> p t d", p=P)).then_inc(mem_in, 16)

            def stream_expert(e, s, arrive):
                for j in range(GROUPS):
                    for n in range(3):
                        k = 3 * j + n
                        slot = k % SLOTS
                        before_j, before_n = divmod((k - SLOTS) % (3 * GROUPS), 3)
                        sp.wait_ge(s[("gate", "up", "down")[before_n]],
                                   GROUPS * e + AHEAD + before_j + 1 - (GROUPS if k < SLOTS else 0))
                        if n < 2:
                            w = io["moe_w_gate" if n == 0 else "moe_w_up"][0]
                            src = w[bass.ds(e, 1), :, j * CHUNK:(j + 1) * CHUNK].rearrange(
                                "e (k p) n -> p (e k) n", p=P)
                            dst = ring[:, slot, :].rearrange("p (k n) -> p k n", k=KB)
                        else:
                            src = io["moe_w_down"][0][bass.ds(e, 1), j * CHUNK:(j + 1) * CHUNK, :].rearrange(
                                "e (k p) n -> p (e k) n", p=P)
                            dst = ring[:, slot, :].rearrange("p (k n) -> p k n", k=4)
                        sp.dma_start(dst, src).then_inc(arrive[slot], 16)

            holder = {}

            def slot_free(slot):
                if slot not in holder:
                    return
                kind, what = freed_by[holder[slot]]
                if kind == "unit":
                    filled(sp, what)
                elif kind == "sum":
                    sp.wait_ge(acc_full, acc_no[what] + 1)
                else:
                    sp.wait_ge(rows_used, what)

            for key, src in chunks:
                if key == "moe":
                    sp.wait_ge(consts_in, CONSTS)
                    filled(sp, ("norm", ("ffn", 1), 0))
                    sp.dma_start(route, io["c_route"]).then_inc(route_in, 16)
                    for slot in range(SLOTS):
                        slot_free(slot)
                    with sp.Fori(0, N_EXPERTS) as e:
                        stream_expert(e, moe_sems[0], landed)
                    holder.clear()
                    sp.wait_ge(moe_sems[0]["down"], GROUPS * N_EXPERTS + AHEAD)
                    over = sp.value_load(flag_i[0:1, 0:1], min_val=0, max_val=1)
                    with sp.If(over > 0):
                        with sp.Fori(0, N_EXPERTS) as e:
                            stream_expert(e, moe_sems[1], ovf_landed)
                        sp.wait_ge(moe_sems[1]["down"], GROUPS * N_EXPERTS + AHEAD)
                    sp.wait_ge(moe_sems[0]["down"], GROUPS * N_EXPERTS + AHEAD)
                    continue
                slot = where[key][0]
                slot_free(slot)
                sp.dma_start(weights(key), src).then_inc(landed[slot], 16)
                holder[slot] = key
                if key[0] in ("pp", "km") or key == ("pg", 1, 0):
                    before(key)
            sp.wait_ge(h_ready, h_at["wo2", 1])
            sp.dma_start(out[0].rearrange("(t p) d -> p t d", p=P), h[:, :, :]).then_inc(out_written, 16)
            sp.wait_ge(out_written, 16)

        @block.tensor
        def _(pe):
            def norm(name):
                pe.wait_ge(xn_ready, norm_no[name] + 1)
                turn_rows(("norm", name), xn, 4)

            def turn_rows(prefix, rows, count):
                for j in range(count):
                    key = (*prefix, j)
                    free_bank(pe, key)
                    for k in range(2):
                        for t in range(NT):
                            last = pe.transpose(bank_of(key)[:, (k * NT + t) * P:(k * NT + t + 1) * P],
                                                rows[:, t, (2 * j + k) * P:(2 * j + k + 1) * P], ident[:, :])
                    last.then_inc(unit_full, 1)

            def features(key, wkey, c0, n=2 * P):
                free_bank(pe, key)
                arrived(pe, wkey)
                w = weights(wkey)
                for b in range((n + P - 1) // P):
                    m = min(P, n - b * P)
                    for k in range(KB):
                        last = pe.matmul(bank_of(key)[0:m, b * SEQ:(b + 1) * SEQ],
                                         w[:, k, c0 + b * P:c0 + b * P + m], xT[:, k, :],
                                         start=(k == 0), stop=(k == KB - 1))
                last.then_inc(unit_full, 1)

            def rows_unit(key, wkey, t, c0=0, n=CHUNK):
                free_bank(pe, key)
                arrived(pe, wkey)
                for k in range(KB):
                    last = pe.matmul(bank_of(key)[:, 0:n], xT[:, k, tok(t)], weights(wkey)[:, k, c0:c0 + n],
                                     start=(k == 0), stop=(k == KB - 1))
                last.then_inc(unit_full, 1)

            def attention(name, l, inputs):
                count, dv, spans = att_shape(name)
                first = att_first[name, l]
                for key in inputs:
                    emptied(pe, key)
                if name == "fox":
                    pe.wait_ge(cum_ready, l + 1)

                def scores(u):
                    g = first + u
                    if g >= 2:
                        pe.wait_ge(att_exp, g - 1)
                    q, k, _ = att_operands(name, u)
                    for t, (c0, n) in enumerate(spans):
                        dst = bank[g % 2][:, c0:c0 + n]
                        last = pe.matmul(dst, q[:, tok(t)], k[:, 0:n], start=True, stop=(name != "fox"))
                        if name == "fox":
                            one = ident[0:HEADS4, u:u + 1]
                            pe.matmul(dst, fox[:, 2, tok(t)], one.to_broadcast([HEADS4, n]), start=False, stop=False)
                            last = pe.matmul(dst, one.to_broadcast([HEADS4, P]), fox[:, 3, 0:n],
                                             start=False, stop=True)
                    last.then_inc(att_scores, 1)

                def turn(u):
                    g = first + u
                    pe.wait_ge(att_exp, g + 1)
                    if g >= 2:
                        pe.wait_ge(att_copied, g - 1)
                    for b in range((spans[1][0] + spans[1][1]) // P):
                        last = pe.transpose(bank[2 + g % 2][:, b * P:(b + 1) * P],
                                            probs[:, g % 2, b * P:(b + 1) * P], ident[:, :])
                    last.then_inc(att_turned, 1)

                def values(u):
                    g = first + u
                    if u == 0 and out_use[name, l]:
                        pe.wait_ge(out_taken, out_use[name, l])
                    pe.wait_ge(att_copied, g + 1)
                    _, _, val = att_operands(name, u)
                    for t, (c0, n) in enumerate(spans):
                        for s in range(n // P):
                            last = pe.matmul(att_out(name, u, t), probsT[:, g % 2, c0 + s * P:c0 + (s + 1) * P],
                                             val[:, s, :], start=(s == 0), stop=(s == n // P - 1))
                    last.then_inc(att_pv, 1)

                for i in range(count + 2):
                    if i < count:
                        scores(i)
                    if 0 <= i - 1 < count:
                        turn(i - 1)
                    if i >= 2:
                        values(i - 2)

            def retention(l):
                for key in (("qcT", l), ("kcT", l)):
                    emptied(pe, key)
                emptied(pe, ("vgc", l, 1))
                pe.wait_ge(out_taken, out_use["ret", l])
                for u in range(HEADS4 + 1):
                    if u < HEADS4:
                        if u >= 2:
                            pe.wait_ge(ret_weights, HEADS4 * l + u - 1)
                        rows, blk = slice(64 * (u % 2), 64 * (u % 2) + 64), 6 + u // 2
                        pe.matmul(bank[u % 2][:, 0:SEQ], kT[rows, blk, 0:P], qT[rows, blk, :], start=True, stop=True)
                        pe.matmul(bank[u % 2][:, SEQ:SEQ + P], kT[rows, blk, tok(1)], qT[rows, blk, tok(1)],
                                  start=True, stop=True).then_inc(ret_scores, 1)
                    if u >= 1:
                        w = u - 1
                        pe.wait_ge(ret_weights, HEADS4 * l + w + 1)
                        src = (probs, probsT)[w // 2][:, w % 2, :]
                        val = v[:, :, 768 + 64 * w:832 + 64 * w]
                        pe.matmul(bank[5][:, w * P:w * P + 64], src[:, 0:P], val[:, 0, :], start=True, stop=True)
                        pe.matmul(bank[5][:, w * P + 64:w * P + P], src[:, P:SEQ], val[:, 0, :],
                                  start=True, stop=False)
                        pe.matmul(bank[5][:, w * P + 64:w * P + P], src[:, SEQ:3 * P], val[:, 1, :],
                                  start=False, stop=True).then_inc(ret_pv, 1)

            def accumulate(key, l, nchunks):
                pe.wait_ge(out_taken, out_use[key, l])
                for c in range(nchunks):
                    arrived(pe, (key, l, c))
                    w = weights((key, l, c))
                    for k in range(4):
                        for t in range(NT):
                            for j in range(2):
                                last = pe.matmul(bank[4 + 2 * t + j][:, :], xT[:, 4 * c + k, tok(t)],
                                                 w[:, k, j * CHUNK:(j + 1) * CHUNK],
                                                 start=(c == 0 and k == 0), stop=(c == nchunks - 1 and k == 3))
                    last.then_inc(acc_full if c == nchunks - 1 else rows_used, 1)

            def dense():
                emptied(pe, ("norm", ("ffn", 0), 3))
                emptied(pe, ("norm", ("ffn", 0), 2))
                pe.wait_ge(out_taken, out_use["ffn", 0])

                def down(f):
                    emptied(pe, ("ff", f))
                    arrived(pe, ("dd", f // 4))
                    w = weights(("dd", f // 4))
                    for t in range(NT):
                        for j in range(2):
                            last = pe.matmul(bank[4 + 2 * t + j][:, :], hTd[:, f % 8, tok(t)],
                                             w[:, f % 4, j * CHUNK:(j + 1) * CHUNK],
                                             start=(f == 0), stop=(f == FB_DENSE - 1))
                    if f == FB_DENSE - 1:
                        last.then_inc(acc_full, 1)
                    elif f % 4 == 3:
                        last.then_inc(rows_used, 1)

                for f in range(FB_DENSE):
                    free_bank(pe, ("ff", f))
                    for n, name in enumerate(("dg", "du")):
                        key = (name, f // 4)
                        arrived(pe, key)
                        for k in range(KB):
                            last = pe.matmul(bank_of(("ff", f))[:, n * SEQ:(n + 1) * SEQ],
                                             weights(key)[:, k, (f % 4) * P:(f % 4 + 1) * P], xT[:, k, :],
                                             start=(k == 0), stop=(k == KB - 1))
                    last.then_inc(unit_full, 1)
                    if f >= 1:
                        down(f - 1)
                down(FB_DENSE - 1)

            def router():
                emptied(pe, ("norm", ("ffn", 1), 3))
                emptied(pe, ("norm", ("ffn", 1), 2))
                free_bank(pe, ("logits",))
                for t in range(NT):
                    for k in range(KB):
                        last = pe.matmul(bank_of(("logits",))[:, t * 8:t * 8 + 8], xT[:, k, tok(t)], rtw[:, k, :],
                                         start=(k == 0), stop=(k == KB - 1))
                last.then_inc(unit_full, 1)
                pe.wait_ge(members_ready, 1)
                pe.wait_ge(route_in, 16)
                free_bank(pe, ("rank",))
                b = bank_of(("rank",))
                pe.matmul(b[:, 0:8], route[:, 0, :], routing[:, 4, 0, :], start=True, stop=True)
                pe.matmul(b[:, 8:16], route[:, 0, :], routing[:, 4, 1, :], start=True, stop=False)
                pe.matmul(b[:, 8:16], route[:, 1, :], routing[:, 4, 0, :], start=False, stop=True).then_inc(unit_full, 1)
                free_bank(pe, ("rank_max",))
                pe.wait_ge(rank_max, 1)
                pe.transpose(bank_of(("rank_max",))[0:1, 0:P], lone[:, 0:1], ident[:, :]).then_inc(unit_full, 1)

            def expert(e, s, arrive, base):
                tn = [0]

                def turn_bank():
                    n = tn[0]
                    tn[0] += 1
                    if n < 2:
                        if n == 0:
                            pe.wait_ge(s["tdve"], 5 * e + 1)
                    elif n - 2 in (2, 10, 11):
                        pe.wait_ge(s["tdve"], 5 * e + {2: 1, 10: 2, 11: 3}[n - 2] + 1)
                    else:
                        pe.wait_ge(s["tact"], 9 * e + (n - 2 + 1 if n - 2 < 2 else n - 2) + 1)
                    return bank[6 + n % 2]

                def slot(n, j):
                    k = 3 * j + n
                    return k % SLOTS, k // SLOTS

                def product(n, j):
                    i, m = slot(n, j)
                    pe.wait_ge(arrive[i], 48 * e + 16 * (base[i] + m) + 16)
                    w = ring[:, i, :].rearrange("p (k n) -> p k n", k=KB)
                    for k in range(KB):
                        last = pe.matmul(bank[2 * n + j % 2][:, :], xg[:, k, :], w[:, k, :],
                                         start=(k == 0), stop=(k == KB - 1))
                    last.then_inc(s[("gate", "up")[n]], 1)

                def turn_hidden(j):
                    b = turn_bank()
                    pe.wait_ge(s["hm"], GROUPS * e + j + 2)
                    for f in range(4):
                        last = pe.transpose(b[:, f * P:(f + 1) * P], hm[:, j % 2, f * P:(f + 1) * P], ident[:, :])
                    last.then_inc(s["tfull"], 1)

                def down(j):
                    if j == 0:
                        pe.wait_ge(s["y"], e + 1)
                    pe.wait_ge(s["tact"], 9 * e + 3 + j + 1)
                    i, m = slot(2, j)
                    pe.wait_ge(arrive[i], 48 * e + 16 * (base[i] + m) + 16)
                    w = ring[:, i, :].rearrange("p (k n) -> p k n", k=4)
                    for f in range(4):
                        for c in range(2):
                            last = pe.matmul(bank[4 + c][:, :], hT[:, j % 2, f, :], w[:, f, c * CHUNK:(c + 1) * CHUNK],
                                             start=(j == 0 and f == 0), stop=(j == GROUPS - 1 and f == 3))
                    last.then_inc(s["down"], 1)

                pe.wait_ge(s["sel"], e + 1)
                for a in range(2):
                    b = turn_bank()
                    for k in range(4):
                        for t in range(NT):
                            last = pe.matmul(b[:, k * P:(k + 1) * P], xn[:, t, (4 * a + k) * P:(4 * a + k + 1) * P],
                                             pickP[:, t, :], start=(t == 0), stop=(t == NT - 1))
                    last.then_inc(s["tfull"], 1)
                b = turn_bank()
                for t in range(NT):
                    last = pe.transpose(b[:, t * P:(t + 1) * P], pickG[:, t, :], ident[:, :])
                last.then_inc(s["tfull"], 1)
                pe.wait_ge(s["tact"], 9 * e + 2 + 1)
                for j in range(GROUPS):
                    if j == 0:
                        pe.wait_ge(s["hm"], GROUPS * e + 1)
                    elif j >= 2:
                        pe.wait_ge(s["hm"], GROUPS * e + j)
                    product(0, j)
                    if j >= 1:
                        turn_hidden(j - 1)
                    product(1, j)
                    if j >= 1:
                        down(j - 1)
                turn_hidden(GROUPS - 1)
                down(GROUPS - 1)
                pe.wait_ge(s["y"], e + 2)
                pe.wait_ge(s["tdve"], 5 * e + 2)
                for t in range(NT):
                    for c in range(2):
                        b = turn_bank()
                        pe.matmul(b[:, :], pickGT[:, tok(t)], yx[:, c * CHUNK:(c + 1) * CHUNK],
                                  start=True, stop=True).then_inc(s["tfull"], 1)

            def prime(s):
                for name in ("gate", "up", "down"):
                    pe.nop().then_inc(s[name], AHEAD)

            def experts():
                router()
                for name in ("logits", "rank", "rank_max"):
                    emptied(pe, (name,))
                pe.wait_ge(out_taken, out_use["wo", 1] + 1)
                prime(moe_sems[0])
                with pe.Fori(0, N_EXPERTS) as e:
                    expert(e, moe_sems[0], landed, moe_base)
                pe.wait_ge(route_ready, 1)
                over = pe.value_load(flag_i[0:1, 0:1], min_val=0, max_val=1)
                with pe.If(over > 0):
                    prime(moe_sems[1])
                    with pe.Fori(0, N_EXPERTS) as e:
                        expert(e, moe_sems[1], ovf_landed, [0] * SLOTS)

            def layer_embedding(l):
                norm(("ple", l))
                pe.wait_ge(p_in, 16 * (l + 1))
                key = ("pT", l)
                free_bank(pe, key)
                for k in range(2):
                    for t in range(NT):
                        last = pe.transpose(bank_of(key)[:, (k * NT + t) * P:(k * NT + t + 1) * P],
                                            pin[:, t, k * P:(k + 1) * P], ident[:, :])
                last.then_inc(unit_full, 1)
                emptied(pe, ("norm", ("ple", l), 3))
                emptied(pe, key)
                arrived(pe, ("pp", l))
                for j in range(2):
                    for t in range(NT):
                        rows_unit(("gate", l, j, t), ("pg", l, j), t)
                        key = ("pproj", l, j, t)
                        free_bank(pe, key)
                        for k in range(2):
                            last = pe.matmul(bank_of(key)[:, :], pT[:, k, tok(t)],
                                             weights(("pp", l))[:, k, j * CHUNK:(j + 1) * CHUNK],
                                             start=(k == 0), stop=(k == 1))
                        last.then_inc(unit_full, 1)

            def hgrn(l):
                emptied(pe, ("ih", l, 1))
                pe.wait_ge(out_taken, out_use["hgrn", l])
                n = (LEVELS + 2) * l

                def heads(dst, s, t):
                    for hd in range(HEADS4):
                        last = pe.matmul(dst[:, hd * P:(hd + 1) * P], kT[:, hd, tok(s)], qT[:, hd, tok(t)],
                                         start=True, stop=True)
                    return last

                for lv in range(LEVELS + 1):
                    pe.wait_ge(hg_qk, n + lv + 1)
                    if lv >= 2:
                        pe.wait_ge(hg_placed, n + lv - 1)
                    for c in range(NT):
                        last = heads(bank[4 + 2 * (lv % 2) + c], c, c)
                    last.then_inc(hg_scores, 1)
                pe.wait_ge(hg_qk, n + LEVELS + 2)
                pe.wait_ge(hg_placed, n + LEVELS)
                heads(bank[4 + 2 * ((LEVELS + 1) % 2)], 0, 1).then_inc(hg_scores, 1)
                pe.wait_ge(hg_placed, n + LEVELS + 2)
                for t in range(NT):
                    for hd in range(HEADS4):
                        dst = bank[4 + t][:, hd * P:(hd + 1) * P]
                        last = pe.matmul(dst, atH[:, t, hd, :], v[:, t, hd * P:(hd + 1) * P],
                                         start=True, stop=(t == 0))
                        if t == 1:
                            last = pe.matmul(dst, atH[:, 2, hd, :], v[:, 0, hd * P:(hd + 1) * P],
                                             start=False, stop=True)
                last.then_inc(hg_pv, 1)

            pe.wait_ge(consts_in, CONSTS)
            for l in range(LAYERS):
                norm(("mix", l))
                emptied(pe, ("norm", ("mix", l), 2))
                emptied(pe, ("norm", ("mix", l), 3))
                for name in ("qa", "ka", "va", "qkb", "vfb", "qkc", "vgc"):
                    for i in range(2):
                        key = (name, l, i)
                        if name in ("qa", "ka", "qkb"):
                            features(key, (name, l), 2 * P * i)
                        elif name == "vfb" and i == 0:
                            free_bank(pe, key)
                            arrived(pe, (name, l))
                            for t in range(NT):
                                for k in range(KB):
                                    last = pe.matmul(bank_of(key)[:, t * 256:(t + 1) * 256], xT[:, k, tok(t)],
                                                     weights((name, l))[:, k, 0:256],
                                                     start=(k == 0), stop=(k == KB - 1))
                            last.then_inc(unit_full, 1)
                        elif name == "vfb":
                            features(key, (name, l), 256, HEADS4)
                        else:
                            rows_unit(key, (name, l), i)
                pe.wait_ge(rotated, l + 1)
                for n, key in enumerate((("qcT", l), ("kcT", l))):
                    free_bank(pe, key)
                    for k in range(2):
                        for t in range(NT):
                            c0 = t * G + (2 * n + k) * P
                            last = pe.transpose(bank_of(key)[:, (k * NT + t) * P:(k * NT + t + 1) * P],
                                                a2[:, c0:c0 + P], ident[:, :])
                    last.then_inc(unit_full, 1)
                emptied(pe, ("qcT", l))
                emptied(pe, ("kcT", l))
                attention("diff", l, [("vgc", l, 1), ("qkc", l, 1)])
                attention("fox", l, [])
                retention(l)
                pe.wait_ge(y_ready, l + 1)
                turn_rows(("yT", l), y1, 4)
                emptied(pe, ("yT", l, 2))
                emptied(pe, ("yT", l, 3))
                accumulate("wo", l, 2)
                norm(("ffn", l))
                if l == 0:
                    dense()
                else:
                    experts()
                layer_embedding(l)
            for l in range(LAYERS):
                norm(("mem", l))
                emptied(pe, ("norm", ("mem", l), 2))
                emptied(pe, ("norm", ("mem", l), 3))
                for name in ("km", "vm"):
                    for i in range(NT):
                        rows_unit((name, l, i), (name, l), i)
                pe.wait_ge(normed, 4 * l + 1)
                turn_rows(("kmT", l), a2[:, :].rearrange("p (t d) -> p t d", t=NT), 2)
                norm(("mix2", l))
                emptied(pe, ("norm", ("mix2", l), 2))
                emptied(pe, ("norm", ("mix2", l), 3))
                for name in ("qm", "qa2", "ka2", "va2"):
                    for i in range(NT):
                        rows_unit((name, l, i), (name, l), i)
                    if name == "qm":
                        pe.wait_ge(normed, 4 * l + 2)
                        turn_rows(("qmT", l), a1[:, :].rearrange("p (t d) -> p t d", t=NT), 2)
                pe.wait_ge(normed, 4 * l + 3)
                turn_rows(("qaT2", l), a1[:, :].rearrange("p (t d) -> p t d", t=NT), 2)
                pe.wait_ge(normed, 4 * l + 4)
                turn_rows(("kaT2", l), a2[:, :].rearrange("p (t d) -> p t d", t=NT), 2)
                emptied(pe, ("kaT2", l, 1))
                attention("moba", l, [("va2", l, 1)])
                attention("memory", l, [])
                for name in ("qh", "fh", "ih"):
                    for i in range(2):
                        if name == "ih":
                            rows_unit((name, l, i), (name, l), i)
                        else:
                            features((name, l, i), (name, l), 2 * P * i)
                hgrn(l)
                for c in range(3):
                    for i in range(NT):
                        rows_unit(("z", l, c, i), ("z", l, c), i)
                pe.wait_ge(y_ready, LAYERS + l + 1)
                turn_rows(("yT2", l), y2, 6)
                emptied(pe, ("yT2", l, 4))
                emptied(pe, ("yT2", l, 5))
                accumulate("wo2", l, 3)

        @block.scalar
        def _(act):
            served = [0]

            def serve(dst, src, func, scale=1.0, bias=0.0):
                served[0] += 1
                act.wait_ge(dve_asks, served[0])
                act.activation(dst, src, func, scale=scale, bias=bias).then_inc(act_answers, 1)

            def serve_sqrt(n):
                serve(stat[:, 1, 0:n], stat[:, 0, 0:n], ACT.Sqrt)

            def norm(name):
                src = norm_input(act, name)
                if norm_no[name]:
                    act.wait_ge(xn_ready, norm_no[name])
                for t in range(NT):
                    last = act.activation(xn[:, t, :], src[:, t, :], ACT.Square, accum_out=ssum[:, t:t + 1])
                last.then_inc(squares, 1)
                serve_sqrt(NT)
                if name != "final":
                    gain = gcols[:, norm_gain[name], :]
                    for j in (0, 2):
                        key = ("norm", name, j)
                        filled(act, key)
                        for k in range(2):
                            last = act.activation(xT[:, 2 * j + k, :], bank_of(key)[:, k * SEQ:(k + 1) * SEQ],
                                                  ACT.Copy, scale=gain[:, 2 * j + k:2 * j + k + 1])
                        last.then_inc(unit_act, 1)

            def take(key, dst, scale=1.0, src=None, func=ACT.Copy):
                filled(act, key)
                act.activation(dst, bank_of(key)[:, :] if src is None else src, func, scale=scale).then_inc(unit_act, 1)

            def flat(tensor, c0, n):
                return tensor[:, c0:c0 + n, :].rearrange("p a b -> p (a b)")

            def attention(name, l):
                count, _, spans = att_shape(name)
                first = att_first[name, l]

                def exps(u):
                    g = first + u
                    act.wait_ge(att_max, g + 1)
                    if g >= 2:
                        act.wait_ge(att_turned, g - 1)
                    for t, (c0, n) in enumerate(spans):
                        i = u * NT + t
                        last = act.activation(probs[:, g % 2, c0:c0 + n], bank[g % 2][:, c0:c0 + n], ACT.Exp,
                                              bias=negmax[:, i:i + 1], accum_out=rowsum[:, i:i + 1])
                    last.then_inc(att_exp, 1)

                def copy(u):
                    g = first + u
                    n = spans[1][0] + spans[1][1]
                    act.wait_ge(att_turned, g + 1)
                    if g >= 2:
                        act.wait_ge(att_pv, g - 1)
                    act.activation(probsT[:, g % 2, 0:n], bank[2 + g % 2][:, 0:n], ACT.Copy).then_inc(att_copied, 1)

                for i in range(count + 1):
                    if i < count:
                        exps(i)
                    if i >= 1:
                        copy(i - 1)

            def expert(e, s):
                act.wait_ge(s["tfull"], 14 * e + 1)
                for a in range(2):
                    if a:
                        act.wait_ge(s["tfull"], 14 * e + 2)
                    for k in range(4):
                        i = 4 * a + k
                        last = act.activation(xg[:, i, :], bank[6 + a][:, k * P:(k + 1) * P], ACT.Copy,
                                              scale=gcols[:, norm_gain["ffn", 1], i:i + 1])
                    last.then_inc(s["tact"], 1)

                def copy(j):
                    n = 3 + j
                    act.wait_ge(s["tfull"], 14 * e + n + 1)
                    act.activation(hT[:, j % 2, :, :].rearrange("p f s -> p (f s)"), bank[6 + n % 2][:, :],
                                   ACT.Copy).then_inc(s["tact"], 1)

                for j in range(GROUPS):
                    if j >= 1:
                        copy(j - 1)
                    act.wait_ge(s["up"], GROUPS * e + j + 1 + AHEAD)
                    act.activation(gated[:, j % 2, :], bank[j % 2][:, :], ACT.Silu).then_inc(s["silu"], 1)
                copy(GROUPS - 1)
                act.wait_ge(s["down"], GROUPS * (e + 1) + AHEAD)
                for c in range(2):
                    last = act.activation(yx[:, c * CHUNK:(c + 1) * CHUNK], bank[4 + c][:, :], ACT.Copy)
                last.then_inc(s["y"], 1)

            def prime(s):
                n = 2 * moe_sems.index(s)
                act.activation(act_marks[:, n:n + 1], ident[:, 0:1], ACT.Copy).then_inc(s["tact"], 1)
                act.activation(act_marks[:, n + 1:n + 2], ident[:, 0:1], ACT.Copy).then_inc(s["y"], 1)

            for dst, src in loads[:-1]:
                act.dma_start(dst, src).then_inc(consts_in, 16)
            act.wait_ge(consts_in, CONSTS)
            serve(lbs[:, 1, 1, :], lbs[:, 1, 0, :], ACT.Sigmoid)
            serve(stat[:, 1, 0:2 * LAYERS], stat[:, 0, 0:2 * LAYERS], ACT.Exp)
            serve(rope[:, 1, :, :], rope[:, 1, :, :], ACT.Sin)
            serve(rope[:, 0, :, :], rope[:, 0, :, :], ACT.Sin)
            for l in range(LAYERS):
                norm(("mix", l))
                for i in range(2):
                    take(("qa", l, i), flat(qT, 2 * i, 2), 0.125)
                for i in range(2):
                    take(("va", l, i), v[:, i, 0:512])
                take(("qkb", l, 0), flat(qT, 4, 2), 0.125)
                serve(fox[:, 1, :], fox[:, 1, :], ACT.Exp, scale=-1.0)
                serve(fox[:, 1, :], fox[:, 1, :], ACT.Ln, bias=1.0)
                for i in range(2):
                    key = ("vgc", l, i)
                    filled(act, key)
                    act.activation(sg[:, i, :], bank_of(key)[:, 256:512], ACT.Silu)
                    act.activation(v[:, i, 768:1024], bank_of(key)[:, 0:256], ACT.Copy).then_inc(unit_act, 1)
                take(("qcT", l), flat(qT, 6, 2))
                take(("kcT", l), flat(kT, 6, 2))
                attention("diff", l)
                serve_sqrt(8)
                attention("fox", l)
                serve_sqrt(8)
                for j in (0, 2):
                    take(("yT", l, j), flat(xT, 2 * j, 2))
                norm(("ffn", l))
                if l == 0:
                    for f in range(FB_DENSE):
                        filled(act, ("ff", f))
                        if f >= 2:
                            emptied(act, ("ff", f - 2))
                        act.activation(gated[:, f % 2, 0:SEQ], bank_of(("ff", f))[:, 0:SEQ],
                                       ACT.Silu).then_inc(silu_done, 1)
                else:
                    serve(routing[:, 5, :, :], routing[:, 5, :, :], ACT.Exp)
                    act.wait_ge(route_ready, 1)
                    prime(moe_sems[0])
                    with act.Fori(0, N_EXPERTS) as e:
                        expert(e, moe_sems[0])
                    over = act.value_load(flag_i[0:1, 0:1], min_val=0, max_val=1)
                    with act.If(over > 0):
                        prime(moe_sems[1])
                        with act.Fori(0, N_EXPERTS) as e:
                            expert(e, moe_sems[1])
                norm(("ple", l))
                take(("pT", l), pT.rearrange("p k s -> p (k s)"))
                for j in range(2):
                    for t in range(NT):
                        n = (l * 2 + j) * NT + t
                        if n >= 2:
                            act.wait_ge(gate_used, n - 1)
                        take(("gate", l, j, t), gatebuf[:, n % 2, :], func=ACT.Sigmoid)
            norm("final")
            for l in range(LAYERS):
                norm(("mem", l))
                for i in range(NT):
                    take(("vm", l, i), v[:, i, 512:1024])
                serve_sqrt(2 * 4)
                for j in range(2):
                    take(("kmT", l, j), flat(kT, 4 + 2 * j, 2))
                norm(("mix2", l))
                serve_sqrt(2 * 4)
                for j in range(2):
                    take(("qmT", l, j), flat(qT, 4 + 2 * j, 2), 128.0 ** -0.5)
                serve_sqrt(2 * 8)
                serve_sqrt(2 * 8)
                for i in range(NT):
                    take(("va2", l, i), v[:, i, 0:512])
                for j in range(2):
                    take(("qaT2", l, j), flat(qT, 2 * j, 2), 0.125)
                for j in range(2):
                    take(("kaT2", l, j), flat(kT, 2 * j, 2))
                attention("moba", l)
                attention("memory", l)
                for i in range(2):
                    take(("qh", l, i), flat(qT, 2 * i, 2), func=ACT.Silu)
                for i in range(2):
                    key = ("fh", l, i)
                    filled(act, key)
                    act.activation(a1[:, i * 512:(i + 1) * 512], bank_of(key)[:, :], ACT.Sigmoid)
                    act.activation(flat(kT, 2 * i, 2), bank_of(key)[:, :], ACT.Sigmoid,
                                   scale=-1.0).then_inc(unit_act, 1)
                for i in range(NT):
                    take(("ih", l, i), v[:, i, 0:512])
                serve_sqrt(8)
                for c in range(3):
                    for t in range(NT):
                        n = (l * 3 + c) * NT + t
                        if n >= 2:
                            act.wait_ge(z_used, n - 1)
                        take(("z", l, c, t), zbuf[:, n % 2, :], func=ACT.Silu)
                for j in (0, 2, 4):
                    take(("yT2", l, j), flat(xT, 2 * j, 2))

        @block.vector
        def _(dve):
            steps, asked = [0], [0]

            mark_no = [0]

            def mark():
                mark_no[0] += 1
                return dve.tensor_copy(marks[:, mark_no[0]:mark_no[0] + 1], ident[:, 0:1])

            def link(ins):
                steps[0] += 1
                ins.then_inc(dve_step, 1)
                dve.wait_ge(dve_step, steps[0])

            def ask(ins):
                asked[0] += 1
                ins.then_inc(dve_asks, 1)
                dve.wait_ge(act_answers, asked[0])

            def rstd(sums, n, scale):
                ask(dve.tensor_scalar(stat[:, 0, 0:n], sums, scale, EPS, ALU.mult, ALU.add))
                link(dve.reciprocal(stat[:, 1, 0:n], stat[:, 1, 0:n]))

            def norm(name):
                src = norm_input(dve, name)
                dve.wait_ge(squares, norm_no[name] + 1)
                rstd(ssum[:, :], NT, 1.0 / D)
                if name == "final":
                    dve.wait_ge(final_in, 16)
                    for t in range(NT):
                        link(dve.tensor_scalar(h[:, t, :], h[:, t, :], stat[:, 1, t:t + 1], None, ALU.mult))
                        last = dve.tensor_tensor(h[:, t, :], h[:, t, :], g_final, ALU.mult)
                    last.then_inc(h_ready, 1)
                    dve.wait_ge(h_ready, h_at["final"])
                    mark().then_inc(xn_ready, 1)
                    return
                for t in range(NT):
                    last = dve.tensor_scalar(xn[:, t, :], src[:, t, :], stat[:, 1, t:t + 1], None, ALU.mult)
                last.then_inc(xn_ready, 1)
                gain = gcols[:, norm_gain[name], :]
                for j in (1, 3):
                    key = ("norm", name, j)
                    filled(dve, key)
                    for k in range(2):
                        last = dve.tensor_scalar(xT[:, 2 * j + k, :], bank_of(key)[:, k * SEQ:(k + 1) * SEQ],
                                                 gain[:, 2 * j + k:2 * j + k + 1], None, ALU.mult)
                    last.then_inc(unit_dve, 1)

            def take(key, dst, src=None):
                filled(dve, key)
                dve.tensor_copy(dst, bank_of(key)[:, :] if src is None else src).then_inc(unit_dve, 1)

            def flat(tensor, c0, n):
                return tensor[:, c0:c0 + n, :].rearrange("p a b -> p (a b)")

            def add_acc(key, l):
                dve.wait_ge(acc_full, acc_no[key, l] + 1)
                for t in range(NT):
                    for j in range(2):
                        cols = slice(j * CHUNK, (j + 1) * CHUNK)
                        last = dve.tensor_tensor(h[:, t, cols], h[:, t, cols], bank[4 + 2 * t + j][:, :], ALU.add)
                last.then_inc(out_taken, 1)
                dve.wait_ge(out_taken, out_use[key, l] + 1)
                mark().then_inc(h_ready, 1)

            def attention(name, l):
                count, _, spans = att_shape(name)
                first = att_first[name, l]
                for u in range(count):
                    g = first + u
                    b = bank[g % 2]
                    dve.wait_ge(att_scores, g + 1)
                    if name != "memory":
                        own = b[:, :].rearrange("p (a c) -> p a c", a=2)[:, :, 0:P]
                        link(dve.tensor_tensor(own, own, causal[:, :].unsqueeze(1).to_broadcast([P, 2, P]), ALU.add))
                    for t, (c0, n) in enumerate(spans):
                        i = u * NT + t
                        last = dve.tensor_reduce(negmax[:, i:i + 1], b[:, c0:c0 + n], AX_X, ALU.max, negate=True)
                    last.then_inc(att_max, 1)
                dve.wait_ge(att_pv, first + count)
                link(dve.reciprocal(rinv[:, 0:count * NT], rowsum[:, 0:count * NT]))

            def per(x, n):
                return x.unsqueeze(len(x.shape)).to_broadcast([*x.shape, n])

            def gained(rows, heads, n, gain):
                r = stat[:, 1, 0:NT * heads].rearrange("p (t h) -> p t h", t=NT)
                link(dve.tensor_tensor(rows, rows, per(r, n), ALU.mult))
                g4 = gain.unsqueeze(1).unsqueeze(1).to_broadcast([P, NT, heads, n])
                return dve.tensor_tensor(rows, rows, g4, ALU.mult)

            def head_squares(rows, heads, n):
                sq = scr[:, 0:NT * heads * n].rearrange("p (t h n) -> p t h n", t=NT, h=heads)
                link(dve.tensor_tensor(sq, rows, rows, ALU.mult))
                link(dve.tensor_reduce(rinv[:, 0:NT * heads], sq, AX_X, ALU.add))
                rstd(rinv[:, 0:NT * heads], NT * heads, 1.0 / n)

            def head_norm(buf, heads, gain):
                n = G // heads
                rows = buf[:, :].rearrange("p (t h n) -> p t h n", t=NT, h=heads)
                head_squares(rows, heads, n)
                return gained(rows, heads, n, gain)

            def rotate(x, heads, off, half, cs, dst):
                x1, x2 = x[:, :, :, off:off + half], x[:, :, :, off + half:off + 2 * half]
                cos, sin = (cs[:, n, :, :].unsqueeze(2).to_broadcast([P, NT, heads, half]) for n in range(2))
                t1 = scr[:, 0:512].rearrange("p (t h n) -> p t h n", t=NT, h=8)[:, :, 0:heads, 0:half]
                t2 = scr[:, 512:1024].rearrange("p (t h n) -> p t h n", t=NT, h=8)[:, :, 0:heads, 0:half]
                t3 = fourth.rearrange("p (t h n) -> p t h n", t=NT, h=8)[:, :, 0:heads, 0:half]
                dve.tensor_tensor(t1, x1, cos, ALU.mult)
                dve.tensor_tensor(t2, x2, sin, ALU.mult)
                link(dve.tensor_tensor(t3, x1, sin, ALU.mult))
                link(dve.tensor_tensor(dst[:, :, :, off:off + half], t1, t2, ALU.subtract))
                link(dve.tensor_tensor(t1, x2, cos, ALU.mult))
                return dve.tensor_tensor(dst[:, :, :, off + half:off + 2 * half], t3, t1, ALU.add)

            fourth = probs[:, 0, :]

            def setup():
                dve.tensor_copy(masks[:, :, :].rearrange("p n t -> p (n t)"), a2[:, :])
                qk = scr[:, 0:512].rearrange("p (n d) -> p n d", n=8)
                for n in range(2):
                    dve.tensor_tensor(scr[:, 512 + 128 * n:640 + 128 * n].rearrange("p (l d) -> p l d", l=2),
                                      qk[:, 4 * n:4 * n + 2, :], qk[:, 4 * n + 2:4 * n + 4, :], ALU.mult)
                link(mark())
                link(dve.tensor_tensor(lbs[:, 1, 0, :], lbs[:, 0, 1, :], lbs[:, 0, 0, :], ALU.subtract))
                ask(mark())
                ask(dve.tensor_reduce(stat[:, 0, 0:4], scr[:, 512:768].rearrange("p (n d) -> p n d", n=4),
                                      AX_X, ALU.add))
                link(dve.tensor_tensor(lam[:, :], stat[:, 1, 0:2], stat[:, 1, 2:4], ALU.subtract))
                for l in range(LAYERS):
                    link(dve.tensor_scalar(lam[:, l:l + 1], lam[:, l:l + 1], lam_init(l), None, ALU.add))
                    link(dve.tensor_scalar(g_subln[:, l, :], g_subln[:, l, :], 1.0 - lam_init(l), None, ALU.mult))
                link(dve.memset(lbs[:, 1, 0, :], 0.0))
                link(dve.tensor_scalar(lbs[:, 0, :, :], lbs[:, 1, :, :], -1.0, 1.0, ALU.mult, ALU.add))
                link(dve.tensor_copy(stat[:, 0, 0:NT], pos_i[:, :]))
                ang = rope[:, 1, :, :]
                turns, part = (scr[:, 16 * n:16 * n + 16].rearrange("p (t n) -> p t n", t=NT) for n in range(2))
                link(dve.tensor_tensor(ang, per(stat[:, 0, 0:NT], ROPE_HALF),
                                       inv_rope[:, :].unsqueeze(1).to_broadcast([P, NT, ROPE_HALF]), ALU.mult))
                link(dve.tensor_scalar(turns, ang, 1.0 / TWO_PI, ROUND, ALU.mult, ALU.add))
                link(dve.tensor_scalar(turns, turns, -ROUND, None, ALU.add))
                for piece in (PI_HI, PI_MID, PI_LO):
                    link(dve.tensor_scalar(part, turns, -piece, None, ALU.mult))
                    link(dve.tensor_tensor(ang, ang, part, ALU.add))
                link(dve.tensor_scalar(ang, ang, 3.1415925, -3.1415925, ALU.min, ALU.max))
                link(dve.tensor_scalar(part, ang, -1.0, None, ALU.mult))
                link(dve.tensor_tensor(part, part, ang, ALU.max))
                ask(dve.tensor_scalar(rope[:, 0, :, :], part, -1.0, math.pi / 2, ALU.mult, ALU.add))
                ask(mark())

            def mixer(l):
                take(("ka", l, 0), flat(kT, 0, 2))
                take(("ka", l, 1), flat(kT, 2, 2))
                take(("qkb", l, 1), flat(kT, 4, 2))
                key = ("vfb", l, 0)
                take(key, v[:, :, 512:768], bank_of(key)[:, :].rearrange("p (t n) -> p t n", t=NT))
                key = ("vfb", l, 1)
                filled(dve, key)
                dve.tensor_scalar(fox[:, 0, :], bank_of(key)[0:HEADS4, 0:SEQ], bforget[:, l:l + 1], None,
                                  ALU.add).then_inc(unit_dve, 1)
                emptied(dve, key)
                link(dve.tensor_scalar(fox[:, 1, :], fox[:, 0, :], -1.0, None, ALU.mult))
                ask(dve.tensor_tensor(fox[:, 1, :], fox[:, 1, :], fox[:, 0, :], ALU.max))
                ask(dve.tensor_scalar(fox[:, 0, :], fox[:, 0, :], 0.0, None, ALU.min))
                link(dve.tensor_tensor(fox[:, 0, :], fox[:, 0, :], fox[:, 1, :], ALU.subtract))
                link(dve.memset(fox[:, 1, :], 1.0))
                link(dve.tensor_tensor_scan(fox[:, 2, :], fox[:, 1, :], fox[:, 0, :], 0.0, ALU.mult, ALU.add))
                dve.tensor_scalar(fox[:, 3, :], fox[:, 2, :], -1.0, None, ALU.mult).then_inc(cum_ready, 1)
                for i in range(NT):
                    take(("qkc", l, i), a1[:, i * G:(i + 1) * G])
                emptied(dve, ("qkc", l, 1))
                rotate(a1[:, :].rearrange("p (t h n) -> p t h n", t=NT, h=8), 8, 0, 32, rot,
                       a2[:, :].rearrange("p (t h n) -> p t h n", t=NT, h=8)).then_inc(rotated, 1)
                attention("diff", l)
                r4 = rinv[:, :].rearrange("p (h n t) -> p h n t", h=4, n=2)
                link(dve.tensor_scalar(r4[:, :, 1, :], r4[:, :, 1, :], lam[:, l:l + 1], None, ALU.mult))
                ya = y1[:, :, 0:512].rearrange("p t (h n) -> p t h n", h=4)
                second = scr[:, :].rearrange("p (t h n) -> p t h n", t=NT, h=4)
                for hd in range(4):
                    o = bank[4 + hd][:, :].rearrange("p (n t d) -> p n t d", n=2, t=NT)
                    dve.tensor_tensor(ya[:, :, hd, :], o[:, 0], per(r4[:, hd, 0, :], P), ALU.mult)
                    last = dve.tensor_tensor(second[:, :, hd, :], o[:, 1], per(r4[:, hd, 1, :], P), ALU.mult)
                last.then_inc(out_taken, 1)
                dve.wait_ge(out_taken, out_use["diff", l] + 1)
                link(dve.tensor_tensor(ya, ya, second, ALU.subtract))
                head_squares(ya, 4, P)
                link(gained(ya, 4, P, g_subln[:, l, :]))
                attention("fox", l)
                dve.tensor_tensor(y1[:, :, 512:768].rearrange("p t (h n) -> p h t n", h=4),
                                  bank[4][:, :].rearrange("p (h t n) -> p h t n", h=4, t=NT),
                                  per(rinv[:, 0:8].rearrange("p (h t) -> p h t", h=4), 64),
                                  ALU.mult).then_inc(out_taken, 1)
                for u in range(HEADS4):
                    dve.wait_ge(ret_scores, HEADS4 * l + u + 1)
                    dve.tensor_tensor((probs, probsT)[u // 2][:, u % 2, 0:3 * P], bank[u % 2][:, 0:3 * P],
                                      decay[:, u, :], ALU.mult).then_inc(ret_weights, 1)
                dve.wait_ge(ret_pv, HEADS4 * (l + 1))
                yc = y1[:, :, 768:1024].rearrange("p t (h n) -> p t h n", h=4)
                dve.tensor_copy(yc.rearrange("p t h n -> p h t n"),
                                bank[5][:, :].rearrange("p (h t n) -> p h t n", h=4, t=NT)).then_inc(out_taken, 1)
                dve.wait_ge(out_taken, out_use["ret", l] + 1)
                link(dve.tensor_reduce(rinv[:, 0:8], yc, AX_X, ALU.add))
                link(dve.tensor_scalar(rinv[:, 0:8], rinv[:, 0:8], 1.0 / 64, None, ALU.mult))
                link(dve.tensor_tensor(yc, yc, per(rinv[:, 0:8].rearrange("p (t h) -> p t h", t=NT), 64),
                                       ALU.subtract))
                head_squares(yc, 4, 64)
                r = stat[:, 1, 0:8].rearrange("p (t h) -> p t h", t=NT)
                link(dve.tensor_tensor(yc, yc, per(r, 64), ALU.mult))
                ycf = y1[:, :, 768:1024]
                link(dve.tensor_tensor(ycf, ycf, g_ret[:, l, :].unsqueeze(1).to_broadcast([P, NT, 256]), ALU.mult))
                emptied(dve, ("vgc", l, 1))
                dve.tensor_tensor(ycf, ycf, sg[:, :, :], ALU.mult).then_inc(y_ready, 1)
                for j in (1, 3):
                    take(("yT", l, j), flat(xT, 2 * j, 2))
                add_acc("wo", l)

            def dense():
                for f in range(FB_DENSE):
                    dve.wait_ge(silu_done, f + 1)
                    dve.tensor_tensor(hTd[:, f % 8, :], gated[:, f % 2, 0:SEQ], bank_of(("ff", f))[:, SEQ:2 * SEQ],
                                      ALU.mult).then_inc(unit_dve, 1)
                add_acc("ffn", 0)

            LG, TOP, GT, EQ, MEM, EX, RANK, CE, CMB, TMP = range(10)

            def routes():
                def r(n):
                    return routing[:, n, :, :]

                def wide(x):
                    return x.to_broadcast([P, NT, N_EXPERTS])

                take(("logits",), r(LG), bank_of(("logits",))[:, 0:16].rearrange("p (t n) -> p t n", t=NT))
                emptied(dve, ("logits",))
                for t in range(NT):
                    link(dve.max(routing[:, TOP, t, :], routing[:, LG, t, :]))
                first, second = wide(routing[:, TOP, :, 0:1]), wide(routing[:, TOP, :, 1:2])
                link(dve.tensor_tensor(r(GT), r(LG), second, ALU.is_gt))
                link(dve.tensor_tensor(r(EQ), r(LG), second, ALU.is_equal))
                link(dve.memset(r(TMP), 1.0))
                for t in range(NT):
                    link(dve.tensor_tensor_scan(routing[:, CE, t, :], routing[:, TMP, t, :], routing[:, EQ, t, :],
                                                0.0, ALU.mult, ALU.add))
                link(dve.tensor_reduce(rinv[:, 0:NT], r(GT), AX_X, ALU.add))
                link(dve.tensor_tensor(r(CE), r(CE), per(rinv[:, 0:NT], N_EXPERTS), ALU.add))
                link(dve.tensor_scalar(r(CE), r(CE), 2.0, None, ALU.is_le))
                link(dve.tensor_tensor(r(EQ), r(EQ), r(CE), ALU.mult))
                dve.tensor_tensor(r(MEM), r(GT), r(EQ), ALU.add).then_inc(members_ready, 1)
                ask(dve.tensor_tensor(r(EX), r(LG), first, ALU.subtract))
                dve.wait_ge(members_ready, 1)
                link(dve.tensor_tensor(r(EX), r(EX), r(MEM), ALU.mult))
                link(dve.tensor_reduce(rinv[:, 0:NT], r(EX), AX_X, ALU.add))
                link(dve.reciprocal(rinv[:, 2:2 + NT], rinv[:, 0:NT]))
                link(dve.tensor_tensor(r(CMB), r(EX), per(rinv[:, 2:2 + NT], N_EXPERTS), ALU.mult))
                key = ("rank",)
                filled(dve, key)
                dve.tensor_scalar(r(RANK), bank_of(key)[:, 0:16].rearrange("p (t n) -> p t n", t=NT), 1.0, None,
                                  ALU.add).then_inc(unit_dve, 1)
                emptied(dve, key)
                link(dve.tensor_tensor(r(RANK), r(RANK), r(MEM), ALU.mult))
                link(dve.tensor_scalar(r(RANK), r(RANK), -1.0, None, ALU.add))
                dve.tensor_reduce(lone[:, 0:1], routing[:, RANK, :, :].rearrange("p t n -> p (t n)"), AX_X,
                                  ALU.max).then_inc(rank_max, 1)
                key = ("rank_max",)
                filled(dve, key)
                dve.tensor_reduce(lone[0:1, 6:7], bank_of(key)[0:1, 0:P], AX_X, ALU.max).then_inc(unit_dve, 1)
                emptied(dve, key)
                link(dve.tensor_scalar(lone[0:1, 7:8], lone[0:1, 6:7], P - 0.5, None, ALU.is_ge))
                dve.tensor_copy(flag_i[0:1, 0:1], lone[0:1, 7:8]).then_inc(route_ready, 1)

            def expert(e, s, first_slot):
                def step(n, ins):
                    ins.then_inc(s["step"], 1)
                    dve.wait_ge(s["step"], 3 * e + n)

                one = bass.ds(e, 1)
                step(1, dve.tensor_copy(pick_place, routing[:, RANK, :, one].rearrange("p t n -> p (t n)")))
                step(2, dve.tensor_copy(pick_gate, routing[:, CMB, :, one].rearrange("p t n -> p (t n)")))
                step(3, dve.tensor_scalar(pick_place, pick_place, -float(first_slot), None, ALU.add))
                for t in range(NT):
                    dve.tensor_scalar(pickP[:, t, :], route[:, 2, :], pick_place[:, t:t + 1], None, ALU.is_equal)
                    last = dve.tensor_scalar(pickG[:, t, :], route[:, 2, :], pick_place[:, t:t + 1],
                                             pick_gate[:, t:t + 1], ALU.is_equal, ALU.mult)
                last.then_inc(s["sel"], 1)
                dve.wait_ge(s["tfull"], 14 * e + 3)
                dve.tensor_copy(pickGT, bank[6][:, 0:SEQ]).then_inc(s["tdve"], 1)
                for j in range(GROUPS):
                    dve.wait_ge(s["silu"], GROUPS * e + j + 1)
                    dve.tensor_tensor(hm[:, j % 2, :], gated[:, j % 2, :], bank[2 + j % 2][:, :],
                                      ALU.mult).then_inc(s["hm"], 1)
                for n in range(4):
                    t, c = n // 2, n % 2
                    cols = slice(c * CHUNK, (c + 1) * CHUNK)
                    dve.wait_ge(s["tfull"], 14 * e + 11 + n)
                    dve.tensor_tensor(h[:, t, cols], h[:, t, cols], bank[6 + n % 2][:, :],
                                      ALU.add).then_inc(s["tdve"], 1)

            pick_place, pick_gate = ssum[:, :], rinv[:, 8:8 + NT]

            def prime(s):
                mark().then_inc(s["tdve"], 1)
                mark().then_inc(s["hm"], 1)

            def experts():
                routes()
                prime(moe_sems[0])
                with dve.Fori(0, N_EXPERTS) as e:
                    expert(e, moe_sems[0], 0)
                dve.wait_ge(route_ready, 1)
                over = dve.value_load(flag_i[0:1, 0:1], min_val=0, max_val=1)
                with dve.If(over > 0):
                    prime(moe_sems[1])
                    with dve.Fori(0, N_EXPERTS) as e:
                        expert(e, moe_sems[1], P)
                dve.wait_ge(moe_sems[0]["tdve"], 5 * N_EXPERTS + 1)
                mark().then_inc(h_ready, 1)

            def layer_embedding(l):
                norm(("ple", l))
                for j in range(2):
                    for t in range(NT):
                        key = ("pproj", l, j, t)
                        n = (l * 2 + j) * NT + t
                        cols = slice(j * CHUNK, (j + 1) * CHUNK)
                        emptied(dve, ("gate", l, j, t))
                        filled(dve, key)
                        product = scr[:, (n % 2) * CHUNK:(n % 2 + 1) * CHUNK]
                        dve.tensor_tensor(product, gatebuf[:, n % 2, :], bank_of(key)[:, :],
                                          ALU.mult).then_inc(unit_dve, 1)
                        emptied(dve, key)
                        last = dve.tensor_tensor(h[:, t, cols], h[:, t, cols], product, ALU.add)
                        last.then_inc(gate_used, 1)
                dve.wait_ge(gate_used, 4 * (l + 1))
                mark().then_inc(h_ready, 1)

            def hgrn(l):
                tot = a1[:, :].rearrange("p (h s) -> p h s", h=HEADS4)
                for i in range(2):
                    emptied(dve, ("fh", l, i))
                for hd in range(HEADS4):
                    dve.tensor_scalar(tot[:, hd, :], tot[:, hd, :], lbs[:, 0, l, hd:hd + 1], lbs[:, 1, l, hd:hd + 1],
                                      ALU.mult, ALU.add)
                    last = dve.tensor_scalar(kT[:, hd, :], kT[:, hd, :], lbs[:, 0, l, hd:hd + 1], None, ALU.mult)
                link(last)
                link(dve.memset(at[:, :], 0.0))
                n = (LEVELS + 2) * l
                qs = qT[:, 0:HEADS4, :].rearrange("p h s -> p (h s)")
                ks = kT[:, 0:HEADS4, :].rearrange("p h s -> p (h s)")
                mark().then_inc(hg_qk, 1)

                def place(lv):
                    m = masks[:, lv, :].unsqueeze(1).to_broadcast([P, HEADS4, P])
                    for c in range(NT):
                        last = dve.copy_predicated(atH[:, c, :, :], m,
                                                   bank[4 + 2 * (lv % 2) + c][:, :].rearrange("p (h t) -> p h t", h=4))
                    last.then_inc(hg_placed, 1)
                    dve.wait_ge(hg_placed, n + lv + 1)

                for lv in range(LEVELS + 1):
                    dve.wait_ge(hg_scores, n + lv + 1)
                    if lv == 0:
                        dve.tensor_tensor(qs, qs, a1[:, :], ALU.mult).then_inc(hg_qk, 1)
                    else:
                        b = 1 << (lv - 1)
                        q4, k4, t4 = (x.rearrange("p (m two b) -> p m two b", two=2, b=b) for x in (qs, ks, a1[:, :]))
                        m = NT * G // (2 * b)
                        dve.tensor_tensor(q4[:, :, 1, :], q4[:, :, 1, :], per(t4[:, :, 0, 0], b), ALU.mult)
                        link(dve.tensor_tensor(k4[:, :, 0, :], k4[:, :, 0, :], per(t4[:, :, 1, 0], b), ALU.mult))
                        dve.tensor_tensor(t4[:, :, 0, 0], t4[:, :, 0, 0], t4[:, :, 1, 0], ALU.mult).then_inc(hg_qk, 1)
                    dve.wait_ge(hg_qk, n + lv + 2)
                    place(lv)
                dve.wait_ge(hg_scores, n + LEVELS + 2)
                dve.tensor_copy(atH[:, 2, :, :], bank[4 + 2 * ((LEVELS + 1) % 2)][:, :].rearrange(
                    "p (h t) -> p h t", h=4)).then_inc(hg_placed, 1)
                dve.wait_ge(hg_pv, l + 1)
                yh = y2[:, :, 512:1024].rearrange("p t (h n) -> p t h n", h=4)
                for t in range(NT):
                    last = dve.tensor_copy(y2[:, t, 512:1024], bank[4 + t][:, :])
                last.then_inc(out_taken, 1)
                dve.wait_ge(out_taken, out_use["hgrn", l] + 1)
                head_squares(yh, 4, P)
                link(gained(yh, 4, P, g_hgrn[:, l, :]))

            dve.wait_ge(consts_in, CONSTS)
            link(dve.memset(lone[:, :], 0.0))
            setup()
            for l in range(LAYERS):
                norm(("mix", l))
                mixer(l)
                norm(("ffn", l))
                if l == 0:
                    dense()
                else:
                    experts()
                layer_embedding(l)
            norm("final")
            for l in range(LAYERS):
                norm(("mem", l))
                for i in range(NT):
                    take(("km", l, i), a2[:, i * G:(i + 1) * G])
                emptied(dve, ("km", l, 1))
                head_norm(a2, 4, g_mem[:, 1, l, :]).then_inc(normed, 1)
                norm(("mix2", l))
                for i in range(NT):
                    take(("qm", l, i), a1[:, i * G:(i + 1) * G])
                emptied(dve, ("qm", l, 1))
                head_norm(a1, 4, g_mem[:, 0, l, :]).then_inc(normed, 1)
                for n, (name, buf) in enumerate((("qa2", a1), ("ka2", a2))):
                    for i in range(NT):
                        take((name, l, i), buf[:, i * G:(i + 1) * G])
                    emptied(dve, (name, l, 1))
                    link(head_norm(buf, 8, g_moba[:, n, l, :]))
                    rows = buf[:, :].rearrange("p (t h n) -> p t h n", t=NT, h=8)
                    rotate(rows, 8, 0, ROPE_HALF, rope, rows).then_inc(normed, 1)
                attention("moba", l)
                for n in range(2):
                    last = dve.tensor_tensor(
                        y2[:, :, 256 * n:256 * n + 256].rearrange("p t (h n) -> p h t n", h=4),
                        bank[4 + n][:, :].rearrange("p (h t n) -> p h t n", h=4, t=NT),
                        per(rinv[:, 8 * n:8 * n + 8].rearrange("p (h t) -> p h t", h=4), 64), ALU.mult)
                last.then_inc(out_taken, 1)
                dve.wait_ge(out_taken, out_use["moba", l] + 1)
                attention("memory", l)
                for n in range(2):
                    last = dve.tensor_tensor(
                        y2[:, :, 1024 + 256 * n:1280 + 256 * n].rearrange("p t (h n) -> p h t n", h=2),
                        bank[6 + n][:, :].rearrange("p (h t n) -> p h t n", h=2, t=NT),
                        per(rinv[:, 4 * n:4 * n + 4].rearrange("p (h t) -> p h t", h=2), P), ALU.mult)
                last.then_inc(out_taken, 1)
                dve.wait_ge(out_taken, out_use["memory", l] + 1)
                hgrn(l)
                for c in range(3):
                    for t in range(NT):
                        n = (l * 3 + c) * NT + t
                        emptied(dve, ("z", l, c, t))
                        cols = slice(c * G, (c + 1) * G)
                        last = dve.tensor_tensor(y2[:, t, cols], y2[:, t, cols], zbuf[:, n % 2, :], ALU.mult)
                        last.then_inc(z_used, 1)
                dve.wait_ge(z_used, 6 * (l + 1))
                mark().then_inc(y_ready, 1)
                for j in (1, 3, 5):
                    take(("yT2", l, j), flat(xT, 2 * j, 2))
                add_acc("wo2", l)


def kernel(**inputs):
    import numpy as _np
    import concourse.bacc as _bacc
    from concourse import mybir as _mybir
    from concourse.bass_utils import run_bass_kernel_spmd as _run

    nc = _bacc.Bacc("TRN2", target_bir_lowering=False, num_devices=1)
    small = ("norm_mix", "norm_ffn", "ple_norm", "norm_g_2", "mem_norm_g_2", "hgrn_lb_logits_2", "b_forget", "positions_2")
    arrays = {name: _np.ascontiguousarray(a) for name, a in inputs.items() if name not in small}
    gains = _np.concatenate([inputs[name] for name in small[:5]], 0)
    arrays["l_gain_columns"] = _np.ascontiguousarray(gains.reshape(len(gains), KB, P).transpose(2, 0, 1))
    arrays["l_bound_logits"] = _np.ascontiguousarray(
        inputs["hgrn_lb_logits_2"].reshape(LAYERS, HEADS4, P).transpose(2, 0, 1))
    arrays["l_forget_bias"] = _np.ascontiguousarray(inputs["b_forget"].T)
    arrays["l_positions"] = _np.ascontiguousarray(inputs["positions_2"].reshape(NT, P).T)
    arrays.update(constants())
    io = {name: nc.dram_tensor(f"in_{name}", a.shape, _mybir.dt.from_np(a.dtype), kind="ExternalInput").ap()
          for name, a in arrays.items()}
    out = nc.dram_tensor("out_x", (1, SEQ, D), _mybir.dt.float32, kind="ExternalOutput").ap()
    program(nc, io, out)
    r = _run(nc, [{f"in_{name}": a for name, a in arrays.items()}], core_ids=[0])
    return r.results[0]["out_x"]
```

```python
import math
from contextlib import ExitStack

import numpy as np

import concourse.bass as bass
from concourse import mybir

F32 = mybir.dt.float32
F32R = mybir.dt.float32r
I32 = mybir.dt.int32
U8 = mybir.dt.uint8
ALU = mybir.AluOpType
ACT = mybir.ActivationFunctionType
AX_X = mybir.AxisListType.X

P = 128
SEQ = 256
NT = SEQ // P
D = 1024
KB = D // P
LAYERS = 2
EPS = 1e-6
NEG = -1e30

DIFF_UNITS = 8
HEADS4 = 4
FF_DENSE = 2816
FB_DENSE = FF_DENSE // P
N_EXPERTS = 8
FF_EXPERT = 3584
CHUNK = 512
GROUPS = FF_EXPERT // CHUNK
G = 512
DMIX = 3 * G
KB2 = DMIX // P
MOBA_HEADS = 8
ROPE_HALF = 8
HALF = KB * CHUNK // 2
RAW = 7
PARTS = 3
PER_EXPERT = 6 * GROUPS
LEVELS = 7

TWO_PI = 2.0 * math.pi
PI_HI = 6.28125
PI_MID = float(np.float32(TWO_PI - PI_HI))
PI_LO = float(TWO_PI - PI_HI - PI_MID)
ROUND = 12582912.0


def expert_order():
    order = []
    for j in range(GROUPS):
        order += [("gate", j, 0), ("gate", j, 1), ("up", j, 0), ("up", j, 1)]
        if j >= 1:
            order += [("down", j - 1, 0), ("down", j - 1, 1)]
    return order + [("down", GROUPS - 1, 0), ("down", GROUPS - 1, 1)]


EXPERT_ORDER = expert_order()


def hidden_at(j, is_last):
    return 5 + j if j < GROUPS - 1 else (11 if is_last else 13)


def lam_init(layer):
    return 0.8 - 0.6 * math.exp(-0.3 * layer)


def constants():
    t = np.arange(P)
    causal = np.where(t[None, :] <= t[:, None], 0.0, NEG).astype(np.float32)
    log_g = np.log1p(-np.exp2(-5.0 - np.arange(HEADS4)))
    diff = t[None, :] - t[:, None]
    decay = np.zeros((P, HEADS4, 3, P), np.float32)
    for h in range(HEADS4):
        same = np.where(diff >= 0, np.exp(np.maximum(diff, 0) * log_g[h]), 0.0)
        decay[:, h, 0] = decay[:, h, 2] = 0.125 * same
        decay[:, h, 1] = 0.125 * np.exp((diff + P) * log_g[h])
    inv = 10000.0 ** (-np.arange(32) / 32.0).astype(np.float32)
    ang = (np.arange(SEQ, dtype=np.float32)[:, None] * inv.astype(np.float32)[None, :]).astype(np.float32)
    rot = np.stack([np.cos(ang), np.sin(ang)]).astype(np.float32).reshape(2, NT, P, 32)
    rot = np.ascontiguousarray(rot.transpose(2, 0, 1, 3))
    masks = np.zeros((P, LEVELS + 1, P), np.float32)
    s, q = t[:, None], t[None, :]
    masks[:, 0] = s == q
    for lv in range(LEVELS):
        b = 1 << lv
        masks[:, lv + 1] = (s // (2 * b) == q // (2 * b)) & (s % (2 * b) < b) & (q % (2 * b) >= b)
    before = (s < q).astype(np.float32)
    slot = np.broadcast_to(t[None, :].astype(np.float32), (P, P))
    route = np.ascontiguousarray(np.stack([before, np.ones((P, P), np.float32), slot], 1))
    inv_rope = (500000.0 ** (-np.arange(ROPE_HALF, dtype=np.float32) / ROPE_HALF)).astype(np.float32)
    inv_rope = np.ascontiguousarray(np.broadcast_to(inv_rope, (P, ROPE_HALF)))
    return {"c_ident": np.eye(P, dtype=np.float32), "c_causal": causal, "c_decay": decay,
            "c_rot": rot, "c_masks": masks, "c_route": route, "c_inv_rope": inv_rope}


def program(nc, io, out, cut=99):
    ctx = ExitStack()
    with ctx:
        place, top = {}, [(nc.sbuf_base + 31) // 32 * 32]

        def sb(name, shape, dt=F32, over=None, skip=0):
            size = int(np.prod(shape[1:])) * (1 if dt == U8 else 4)
            if over is None:
                place[name] = top[0]
                top[0] += (size + 31) // 32 * 32
            else:
                place[name] = place[over] + skip
            return nc.alloc_sbuf_tensor_at(name, shape, dt, offset=place[name])

        def sem(name):
            return ctx.enter_context(nc.semaphore(name))

        raw = sb("raw", [P, RAW, HALF])
        high = sb("high", [P, PARTS, HALF], F32R)
        low = sb("low", [P, PARTS, HALF], F32R)
        h = sb("h", [P, NT, D])
        yf = sb("yf", [P, NT * DMIX])
        xn = yf[:, 0:NT * D].rearrange("p (t d) -> p t d", t=NT)
        y1 = xn
        y2 = yf[:, :].rearrange("p (t d) -> p t d", t=NT)
        fox = yf[0:HEADS4, NT * D:NT * DMIX].rearrange("p (r s) -> p r s", r=4)
        xT_hi = sb("xT_hi", [P, KB, SEQ], F32R)
        xT_lo = sb("xT_lo", [P, KB, SEQ], F32R)
        mem_src = sb("mem_src", [P, NT, D], over="xT_lo")
        a1 = sb("a1", [P, NT * G])
        a2 = sb("a2", [P, NT * G])
        qT = sb("qT", [P, 8, SEQ])
        kT = sb("kT", [P, 8, SEQ])
        v = sb("v", [P, NT, D])
        at = sb("at", [P, 12 * P])
        decay = at[:, :].rearrange("p (h m) -> p h m", h=HEADS4)
        atH = at[:, :].rearrange("p (b h t) -> p b h t", b=3, h=HEADS4)
        probs = sb("probs", [P, 2, 512])
        probsT = sb("probsT", [P, 2, 512])
        scr = sb("scr", [P, NT * G])
        sg = sb("sg", [P, NT, 256])
        ident = sb("ident", [P, P])
        causal = sb("causal", [P, P])
        masks = sb("masks", [P, LEVELS + 1, P], U8)
        rot = sb("rot", [P, 2, NT, 32])
        gcols = sb("gcols", [P, 10, KB])
        g_subln = sb("g_subln", [P, LAYERS, P])
        g_ret = sb("g_ret", [P, LAYERS, 256])
        g_moba = sb("g_moba", [P, 2, LAYERS, 64])
        g_hgrn = sb("g_hgrn", [P, LAYERS, P])
        g_mem = sb("g_mem", [P, 2, LAYERS, P])
        bforget = sb("bforget", [HEADS4, LAYERS])
        rope = sb("rope", [P, 2, NT, ROPE_HALF])
        inv_rope = sb("inv_rope", [P, ROPE_HALF])
        pos_i = sb("pos_i", [P, NT], I32)
        lbs = sb("lbs", [P, 2, LAYERS, HEADS4])
        lam = sb("lam", [P, LAYERS])
        stat = sb("stat", [P, 2, 16])
        ssum = sb("ssum", [P, NT])
        rowsum = sb("rowsum", [P, 8 * NT])
        negmax = sb("negmax", [P, 8 * NT])
        rinv = sb("rinv", [P, 8 * NT])
        routing = sb("routing", [P, 10, NT, N_EXPERTS])
        forget_rows = sb("forget_rows", [P, NT, HEADS4])
        rtw = sb("rtw", [P, KB, N_EXPERTS])
        lone = sb("lone", [P, 8])
        marks = sb("marks", [P, 32])
        flag_i = sb("flag_i", [1, 1], I32)
        bank = [ctx.enter_context(nc.psum_tensor(f"bank{i}", [P, 512], F32)) for i in range(8)]

        xg_hi = sb("xg_hi", [P, KB, P], F32R, over="qT")
        xg_lo = sb("xg_lo", [P, KB, P], F32R, over="qT", skip=4096)
        yT_hi = sb("yT_hi", [P, KB2 - KB, SEQ], F32R, over="qT")
        yT_lo = sb("yT_lo", [P, KB2 - KB, SEQ], F32R, over="qT", skip=4096)
        hT_hi = sb("hT_hi", [P, 2, 512], F32R, over="kT")
        hT_lo = sb("hT_lo", [P, 2, 512], F32R, over="kT", skip=4096)
        hm = v[:, 0, :].rearrange("p (r n) -> p r n", r=2)
        gated = v[:, 1, :].rearrange("p (r n) -> p r n", r=2)
        pickP = probs[:, 0, 0:256].rearrange("p (t s) -> p t s", t=NT)
        pickG = probs[:, 0, 256:512].rearrange("p (t s) -> p t s", t=NT)
        pickGT = probs[:, 1, :].rearrange("p (r n) -> p r n", r=2)
        yx = scr
        route = a1[:, 0:3 * P].rearrange("p (r s) -> p r s", r=3)
        g_final = a2[:, :]
        pin = a1[:, 512:1024].rearrange("p (t d) -> p t d", t=NT)
        pT_hi = sb("pT_hi", [P, 2, SEQ], F32R, over="probsT")
        pT_lo = sb("pT_lo", [P, 2, SEQ], F32R, over="probsT", skip=2048)
        gatebuf = probs

        def projected(j, t):
            return v[:, t, j * CHUNK:(j + 1) * CHUNK]

        zbuf = probs

        landed = [sem(f"slot{i}_landed") for i in range(RAW)]
        high_done, low_done, pieces_used = sem("high_parts_done"), sem("low_parts_done"), sem("pieces_used")
        high_rows = sem("high_rows_taken")
        first_in = sem("first_in")
        consts_in, p_in, route_in, mem_in = sem("consts_in"), sem("p_in"), sem("route_in"), sem("mem_in")
        final_in, out_written = sem("final_in"), sem("out_written")
        unit_full, unit_act, unit_dve = sem("unit_full"), sem("unit_taken_act"), sem("unit_taken_dve")
        act_step, dve_step = sem("act_step"), sem("dve_step")
        dve_asks, act_answers = sem("dve_asks"), sem("act_answers")
        setup_dve, squares = sem("setup_dve"), sem("squares_summed")
        xn_ready, h_ready = sem("xn_ready"), sem("h_ready")
        att_scores, att_max, att_exp = sem("att_scores"), sem("att_max"), sem("att_exp")
        att_turned, att_copied, att_pv = sem("att_turned"), sem("att_copied"), sem("att_pv")
        cum_ready, rotated, normed = sem("cum_ready"), sem("rotated"), sem("heads_normed")
        ret_scores, ret_weights, ret_pv = sem("ret_scores"), sem("ret_weights"), sem("ret_pv")
        out_taken, y_ready = sem("out_banks_taken"), sem("y_ready")
        hid_high, hid_ready = sem("hidden_high_ready"), sem("hidden_ready")
        z_used, gate_used = sem("z_used"), sem("gate_used")
        hg_qk, hg_scores, hg_pv = sem("hg_qk_ready"), sem("hg_scores"), sem("hg_pv")
        hg_placed = sem("hg_scores_placed")
        members_ready, rank_max, route_ready = sem("members_ready"), sem("rank_max_ready"), sem("route_ready")
        moe_names = ("sel", "tfull", "thigh", "tfree", "silu", "hm", "y", "step")
        moe_sems = [{n: sem(f"moe{p}_{n}") for n in moe_names} for p in range(2)]
        moe_sems[0].update(high=high_done, low=low_done, used=pieces_used, landed=landed)
        moe_sems[1].update(high=sem("high_parts_done_overflow"), low=sem("low_parts_done_overflow"),
                           used=sem("pieces_used_overflow"),
                           landed=[sem(f"slot{i}_landed_overflow") for i in range(RAW)])

        stream, pieces_of, piece_size = [], {}, []
        raw_slot, part_slot, raw_loads, landings = [], [], [0] * RAW, []
        offset = [0]
        units, unit_at, unit_signal = [], {}, {}
        owner_count = {"act": 0, "dve": 0}
        full_count = [0]

        def chunk(key, sources):
            pieces_of[key] = list(range(len(raw_slot), len(raw_slot) + len(sources)))
            for src in sources:
                n = len(raw_slot) + offset[0]
                raw_slot.append(n % RAW)
                part_slot.append(n % PARTS)
                raw_loads[n % RAW] += 1
                landings.append(raw_loads[n % RAW])
                piece_size.append((src.shape[1], src.shape[2]))
                stream.append((len(raw_slot) - 1, key, src))

        def unit(key, owner, piece=None):
            owner_count[owner] += 1
            unit_at[key] = (len(units), owner, owner_count[owner])
            units.append(key)
            if piece is None:
                full_count[0] += 1
                unit_signal[key] = (unit_full, full_count[0])
            else:
                unit_signal[key] = (pieces_used, piece + 1)

        def cols_of(w, c0, n):
            return w[:, c0:c0 + n].rearrange("(k p) n -> p k n", p=P)

        def deep(w, c0, n):
            src = cols_of(w, c0, n)
            return [src[:, 0:KB // 2, :], src[:, KB // 2:KB, :]]

        def wide(w, c0, n):
            return [cols_of(w, c0 + i, 256) for i in range(0, n, 256)]

        def rows_of(w, k0, nk):
            return [w[k * P:(k + 2) * P, :].rearrange("(k p) n -> p k n", p=P) for k in range(k0, k0 + nk, 2)]

        norm_no = {}

        def plan_norm(name):
            norm_no[name] = len(norm_no)
            for j in range(4):
                unit(("norm", name, j), "dve")

        MIX1 = (("qa", 0, 512, "act", "act"), ("ka", 512, 512, "dve", "dve"), ("va", 1024, 512, "act", "act"),
                ("qkb", 1536, 512, "act", "dve"), ("vfb", 2048, 260, "dve", "dve"),
                ("qkc", 2308, 512, "dve", "dve"), ("vgc", 2820, 512, "act", "act"))
        for l in range(LAYERS):
            plan_norm(("mix", l))
            for name, c0, w, own0, own1 in MIX1:
                chunk((name, l), (wide if name in ("qa", "ka", "qkb") else deep)(io["w_in"][l], c0, w))
                for i, owner in enumerate((own0, own1)):
                    p = pieces_of[name, l]
                    unit((name, l, i), owner, p[i] if name in ("qa", "ka", "qkb") else p[1])
            unit(("forgetT", l), "dve")
            unit(("qcT", l), "act")
            unit(("kcT", l), "act")
            for j in range(4):
                unit(("yT", l, j), "dve")
            chunk(("wo", l), rows_of(io["w_out"][l], 0, KB))
            plan_norm(("ffn", l))
            if l == 0:
                wg, wu, wd = io["dense_w_gate"][0], io["dense_w_up"][0], io["dense_w_down"][0]
                for j in range(FB_DENSE // 2):
                    for n, (name, w) in enumerate((("dg", wg), ("du", wu))):
                        chunk((name, j), [cols_of(w, 2 * j * P, 2 * P)])
                        unit((name, j), ("act", "dve")[n], pieces_of[name, j][0])
                    if j >= 1:
                        chunk(("dd", j - 1), rows_of(wd, 2 * j - 2, 2))
                chunk(("dd", FB_DENSE // 2 - 1), rows_of(wd, FB_DENSE - 2, 2))
            else:
                for name in ("logits", "rank", "rank_max"):
                    unit((name,), "dve")
                offset[0] += -(len(raw_slot) + offset[0]) % (RAW * PARTS)
                assert PER_EXPERT % (RAW * PARTS) == 0
                moe_first = len(raw_slot)
                moe_landed = list(raw_loads)
                stream.append((None, "moe", None))
                for n in range(N_EXPERTS * PER_EXPERT):
                    raw_slot.append(n % RAW)
                    part_slot.append(n % PARTS)
                    raw_loads[n % RAW] += 1
                    landings.append(raw_loads[n % RAW])
                    piece_size.append(None)
            plan_norm(("ple", l))
            unit(("pT", l), "dve")
            chunk(("pp", l), rows_of(io["ple_proj"][l], 0, 2))
            for j in range(2):
                for t in range(NT):
                    unit(("pproj", l, j, t), "act", pieces_of["pp", l][0] if (j, t) == (1, 1) else None)
            for j in range(2):
                chunk(("pg", l, j), deep(io["ple_gate"][l], j * CHUNK, CHUNK))
                for t in range(NT):
                    unit(("gate", l, j, t), "act", pieces_of["pg", l, j][1])
        norm_no["final"] = len(norm_no)
        for l in range(LAYERS):
            w2, wm = io["w_in_2"][l], io["w_mem_kv_2"][l]
            plan_norm(("mem", l))
            for n, name in enumerate(("km", "vm")):
                chunk((name, l), deep(wm, n * G, G))
                for i in range(NT):
                    unit((name, l, i), "dve" if name == "km" else "act", pieces_of[name, l][1])
            for j in range(2):
                unit(("kmT", l, j), "act")
            plan_norm(("mix2", l))
            for name, n in (("qm", 6), ("qa2", 0), ("ka2", 1), ("va2", 2)):
                chunk((name, l), deep(w2, n * G, G))
                for i in range(NT):
                    unit((name, l, i), "act" if name == "va2" else "dve", pieces_of[name, l][1])
                if name == "qm":
                    for j in range(2):
                        unit(("qmT", l, j), "act")
            for name in ("qaT2", "kaT2"):
                for j in range(2):
                    unit((name, l, j), "act")
            for name, n in (("qh", 3), ("fh", 4), ("ih", 5)):
                chunk((name, l), (deep if name == "ih" else wide)(w2, n * G, G))
                for i in range(2):
                    unit((name, l, i), "act", pieces_of[name, l][1 if name == "ih" else i])
            for c in range(3):
                chunk(("z", l, c), deep(w2, (7 + c) * G, G))
                for i in range(NT):
                    unit(("z", l, c, i), "act", pieces_of["z", l, c][1])
            for j in range(6):
                unit(("yT2", l, j), "dve")
            chunk(("wo2", l), rows_of(io["w_out_2"][l], 0, KB2))

        att_first, att_n, out_use = {}, 0, {}
        for l in range(LAYERS):
            for name, n in (("diff", 8), ("fox", 4)):
                att_first[name, l], att_n = att_n, att_n + n
                out_use[name, l] = len(out_use)
            out_use["ret", l] = len(out_use)
            out_use["wo", l] = len(out_use)
            if l == 0:
                out_use["ffn", 0] = len(out_use)
        for l in range(LAYERS):
            for name, n in (("moba", 8), ("memory", 4)):
                att_first[name, l], att_n = att_n, att_n + n
                out_use[name, l] = len(out_use)
            out_use["hgrn", l] = len(out_use)
            out_use["wo2", l] = len(out_use)
        last_piece = {("wo", l): pieces_of["wo", l][-1] for l in range(LAYERS)}
        last_piece.update({("wo2", l): pieces_of["wo2", l][-1] for l in range(LAYERS)})
        last_piece["ffn", 0] = pieces_of["dd", FB_DENSE // 2 - 1][0]
        h_at = {key: n + 1 for n, key in enumerate([("wo", 0), ("ffn", 0), ("ple", 0), ("wo", 1), ("ffn", 1),
                                                    ("ple", 1), "final", ("wo2", 0), ("wo2", 1)])}
        norm_src = {("ffn", 0): ("wo", 0), ("ple", 0): ("ffn", 0), ("mix", 1): ("ple", 0), ("ffn", 1): ("wo", 1),
                    ("ple", 1): ("ffn", 1), "final": ("ple", 1), ("mix2", 0): "final", ("mix2", 1): ("wo2", 0)}
        norm_gain = {("mix", 0): 0, ("mix", 1): 1, ("ffn", 0): 2, ("ffn", 1): 3, ("ple", 0): 4, ("ple", 1): 5,
                     ("mix2", 0): 6, ("mix2", 1): 7, ("mem", 0): 8, ("mem", 1): 9}

        def parts(piece):
            k, n = piece_size[piece]
            return tuple(x[:, part_slot[piece], 0:k * n].rearrange("p (k n) -> p k n", k=k) for x in (high, low))

        def bank_of(key):
            return bank[unit_at[key][0] % 4]

        def filled(eng, key):
            eng.wait_ge(*unit_signal[key])

        def emptied(eng, key):
            _, owner, n = unit_at[key]
            eng.wait_ge(unit_act if owner == "act" else unit_dve, n)

        def free_bank(pe, key):
            n = unit_at[key][0]
            if n >= 4:
                emptied(pe, units[n - 4])

        def tok(i):
            return slice(i * P, (i + 1) * P)

        def norm_input(eng, name):
            if name[0] == "mem":
                eng.wait_ge(mem_in, 16 * (name[1] + 1))
                return mem_src
            if name in norm_src:
                eng.wait_ge(h_ready, h_at[norm_src[name]])
            else:
                eng.wait_ge(first_in, FIRST)
            return h

        def att_shape(name):
            if name == "memory":
                return 4, 128, ((0, 256), (256, 256))
            return {"diff": 8, "fox": 4, "moba": 8}[name], 128 if name == "diff" else 64, ((0, 128), (128, 256))

        def att_operands(name, u):
            if name == "memory":
                return qT[:, 4 + u, :], kT[:, 4 + u, :], v[:, :, 512 + 128 * u:640 + 128 * u]
            blk = {"diff": 0, "fox": 4, "moba": 0}[name] + u // 2
            rows = slice(64 * (u % 2), 64 * (u % 2) + 64)
            val = {"diff": slice(128 * (u // 2), 128 * (u // 2) + 128), "fox": slice(512 + 64 * u, 576 + 64 * u),
                   "moba": slice(64 * u, 64 * u + 64)}[name]
            return qT[rows, blk, :], kT[rows, blk, :], v[:, :, val]

        def att_out(name, u, t):
            n, dv, _ = att_shape(name)
            col = (u * NT + t) * dv
            first = {"diff": 4, "fox": 4, "moba": 4, "memory": 6}[name]
            return bank[first + col // 512][:, col % 512:col % 512 + dv]

        def spread(vec, shape):
            return vec.partition_broadcast(P)

        first_loads = [(ident[:, :], io["c_ident"]), (gcols[:, :, :], io["l_gain_columns"]),
                       (h[:, :, :], io["x"][0].rearrange("(t p) d -> p t d", p=P))]
        loads = [(causal[:, :], io["c_causal"]),
                 (decay, io["c_decay"].rearrange("p h b t -> p h (b t)")),
                 (rot[:, :, :, :], io["c_rot"]), (a2[:, :], io["c_masks"].rearrange("p n t -> p (n t)")),
                 (inv_rope[:, :], io["c_inv_rope"]),
                 (pos_i[:, :], io["l_positions"])]
        loads.append((lbs[:, 0, :, :], io["l_bound_logits"]))
        loads.append((bforget[:, :], io["l_forget_bias"]))
        for l in range(LAYERS):
            loads.append((g_subln[:, l, :], io["diff_subln"][l].partition_broadcast(P)))
            loads.append((g_ret[:, l, :], io["ret_gn"][l].partition_broadcast(P)))
            loads.append((g_moba[:, 0, l, :], io["moba_q_norm_2"][l].partition_broadcast(P)))
            loads.append((g_moba[:, 1, l, :], io["moba_k_norm_2"][l].partition_broadcast(P)))
            loads.append((g_hgrn[:, l, :], io["hgrn_o_norm_2"][l].partition_broadcast(P)))
            loads.append((g_mem[:, 0, l, :], io["mem_q_norm_2"][l].partition_broadcast(P)))
            loads.append((g_mem[:, 1, l, :], io["mem_k_norm_2"][l].partition_broadcast(P)))
            for n, name in enumerate(("lambda_q1", "lambda_k1", "lambda_q2", "lambda_k2")):
                at0 = (n * LAYERS + l) * 64
                loads.append((scr[:, at0:at0 + 64], io[name][l].partition_broadcast(P)))
        loads.append((rtw[:, :, :], io["router"][0].rearrange("(k p) n -> p k n", p=P)))
        FIRST = 16 * len(first_loads)
        CONSTS = 16 * len(loads)

        block = ctx.enter_context(nc.Block())

        @block.sync
        def _(sp):
            for dst, src in first_loads[-1:]:
                sp.dma_start(dst, src).then_inc(first_in, 16)

            def stream_expert(e, s, first, loads0):
                for k, (what, j, half) in enumerate(EXPERT_ORDER):
                    slot = k % RAW
                    sp.wait_ge(s["low"], first + PER_EXPERT * e + k - RAW + 1)
                    if what == "down":
                        r0 = j * CHUNK + half * 2 * P
                        src = io["moe_w_down"][0][bass.ds(e, 1), r0:r0 + 2 * P, :].rearrange(
                            "e (k p) n -> p (e k) n", p=P)
                        dst = raw[:, slot, :].rearrange("p (k n) -> p k n", k=2)
                    else:
                        w = io["moe_w_gate" if what == "gate" else "moe_w_up"][0]
                        r0 = half * (D // 2)
                        src = w[bass.ds(e, 1), r0:r0 + D // 2, j * CHUNK:(j + 1) * CHUNK].rearrange(
                            "e (k p) n -> p (e k) n", p=P)
                        dst = raw[:, slot, :].rearrange("p (k n) -> p k n", k=4)
                    sp.dma_start(dst, src).then_inc(s["landed"][slot], 16)

            holder = {}

            def load_p(l):
                sp.dma_start(pin, io["p"][l, 0].rearrange("(t p) d -> p t d", p=P)).then_inc(p_in, 16)

            for piece, key, src in stream:
                if key == "moe":
                    sp.wait_ge(consts_in, CONSTS)
                    filled(sp, ("norm", ("ffn", 1), 0))
                    sp.dma_start(route, io["c_route"]).then_inc(route_in, 16)
                    filled(sp, ("pT", 0))
                    load_p(1)
                    sp.dma_start(g_final, io["final_norm"].partition_broadcast(P)).then_inc(final_in, 16)
                    sp.wait_ge(low_done, moe_first)
                    with sp.Fori(0, N_EXPERTS) as e:
                        stream_expert(e, moe_sems[0], moe_first, moe_landed)
                    sp.wait_ge(pieces_used, moe_first + N_EXPERTS * PER_EXPERT)
                    over = sp.value_load(flag_i[0:1, 0:1], min_val=0, max_val=1)
                    with sp.If(over > 0):
                        with sp.Fori(0, N_EXPERTS) as e:
                            stream_expert(e, moe_sems[1], RAW, [0] * RAW)
                        sp.wait_ge(moe_sems[1]["low"], RAW + N_EXPERTS * PER_EXPERT)
                    for n in range(N_EXPERTS * PER_EXPERT):
                        holder[n % RAW] = moe_first + n
                    sp.wait_ge(pieces_used, moe_first + N_EXPERTS * PER_EXPERT)
                    continue
                if key == ("dd", 0):
                    filled(sp, ("norm", ("ffn", 0), 0))
                    load_p(0)
                if key[0] == "vm" and piece == pieces_of[key][0]:
                    l = key[1]
                    filled(sp, ("gate", 1, 1, 1)) if l == 0 else sp.wait_ge(pieces_used, last_piece["wo2", 0] + 1)
                    sp.dma_start(mem_src[:, :, :], io["mem_2"][0].rearrange("(t p) d -> p t d", p=P)).then_inc(mem_in, 16)
                slot = raw_slot[piece]
                if piece == RAW:
                    for dst, source in loads:
                        sp.dma_start(dst, source).then_inc(consts_in, 16)
                if slot in holder:
                    sp.wait_ge(low_done, holder[slot] + 1)
                k, n = piece_size[piece]
                sp.dma_start(raw[:, slot, 0:k * n].rearrange("p (k n) -> p k n", k=k), src).then_inc(landed[slot], 16)
                holder[slot] = piece
            sp.wait_ge(h_ready, h_at["wo2", 1])
            sp.dma_start(out[0].rearrange("(t p) d -> p t d", p=P), h[:, :, :]).then_inc(out_written, 16)
            sp.wait_ge(out_written, 16)

        @block.tensor
        def _(pe):
            def norm(name):
                pe.wait_ge(xn_ready, norm_no[name] + 1)
                turn_rows(("norm", name), xn, 4)

            def turn_rows(prefix, rows, count):
                for j in range(count):
                    key = (*prefix, j)
                    free_bank(pe, key)
                    for k in range(2):
                        for t in range(NT):
                            last = pe.transpose(bank_of(key)[:, (k * NT + t) * P:(k * NT + t + 1) * P],
                                                rows[:, t, (2 * j + k) * P:(2 * j + k + 1) * P], ident[:, :])
                    last.then_inc(unit_full, 1)

            def exact(dst, stationary, moving, start, stop):
                pe.matmul(dst, stationary[0], moving[0], start=start, stop=False)
                pe.matmul(dst, stationary[0], moving[1], start=False, stop=False)
                return pe.matmul(dst, stationary[1], moving[0], start=False, stop=stop)

            def x_parts(k, cols):
                return xT_hi[:, k, cols], xT_lo[:, k, cols]

            def ready(piece):
                pe.wait_ge(low_done, piece + 1)

            def features(keys, wkey):
                for key, piece in zip(keys, pieces_of[wkey]):
                    free_bank(pe, key)
                    ready(piece)
                    w = parts(piece)
                    for b in range(2):
                        for k in range(KB):
                            last = exact(bank_of(key)[:, b * SEQ:(b + 1) * SEQ],
                                         [x[:, k, b * P:(b + 1) * P] for x in w], x_parts(k, slice(0, SEQ)),
                                         k == 0, k == KB - 1)
                    last.then_inc(pieces_used, 1)

            def rows_units(keys, wkey):
                for half, piece in enumerate(pieces_of[wkey]):
                    for t, key in enumerate(keys):
                        if half == 0:
                            free_bank(pe, key)
                        ready(piece)
                        w = parts(piece)
                        for k in range(KB // 2):
                            kk = half * (KB // 2) + k
                            last = exact(bank_of(key)[:, 0:piece_size[piece][1]], x_parts(kk, tok(t)),
                                         [x[:, k, :] for x in w], kk == 0, kk == KB - 1)
                    last.then_inc(pieces_used, 1)

            def attention(name, l, inputs):
                count, dv, spans = att_shape(name)
                first = att_first[name, l]
                for key in inputs:
                    emptied(pe, key)
                if name == "fox":
                    pe.wait_ge(cum_ready, l + 1)

                def scores(u):
                    g = first + u
                    if g >= 2:
                        pe.wait_ge(att_exp, g - 1)
                    q, k, _ = att_operands(name, u)
                    for t, (c0, n) in enumerate(spans):
                        if name == "memory":
                            last = pe.matmul(bank[g % 2][:, c0:c0 + n], q[:, tok(t)], k[:, 0:n], start=True, stop=True)
                            continue
                        for s in range(t + 1):
                            dst = bank[g % 2][:, c0 + s * P:c0 + (s + 1) * P]
                            last = pe.matmul(dst, q[:, tok(t)], k[:, tok(s)], start=True,
                                             stop=(name != "fox" and s < t))
                            if name == "fox":
                                one = ident[0:HEADS4, u:u + 1].to_broadcast([HEADS4, P])
                                pe.matmul(dst, fox[:, 2, tok(t)], one, start=False, stop=False)
                                last = pe.matmul(dst, one, fox[:, 3, tok(s)], start=False, stop=(s < t))
                            if s == t:
                                last = pe.matmul(dst, ident[:, :], causal[:, :], start=False, stop=True)
                    last.then_inc(att_scores, 1)

                def turn(u):
                    g = first + u
                    pe.wait_ge(att_exp, g + 1)
                    if g >= 2:
                        pe.wait_ge(att_copied, g - 1)
                    for b in range((spans[1][0] + spans[1][1]) // P):
                        last = pe.transpose(bank[2 + g % 2][:, b * P:(b + 1) * P],
                                            probs[:, g % 2, b * P:(b + 1) * P], ident[:, :])
                    last.then_inc(att_turned, 1)

                def values(u):
                    g = first + u
                    if u == 0 and out_use[name, l]:
                        pe.wait_ge(out_taken, out_use[name, l])
                    pe.wait_ge(att_copied, g + 1)
                    _, _, val = att_operands(name, u)
                    for t, (c0, n) in enumerate(spans):
                        for s in range(n // P):
                            last = pe.matmul(att_out(name, u, t), probsT[:, g % 2, c0 + s * P:c0 + (s + 1) * P],
                                             val[:, s, :], start=(s == 0), stop=(s == n // P - 1))
                    last.then_inc(att_pv, 1)

                for i in range(count + 2):
                    if i < count:
                        scores(i)
                    if 0 <= i - 1 < count:
                        turn(i - 1)
                    if i >= 2:
                        values(i - 2)

            def retention(l):
                for key in (("qcT", l), ("kcT", l)):
                    emptied(pe, key)
                emptied(pe, ("vgc", l, 1))
                pe.wait_ge(out_taken, out_use["ret", l])
                for u in range(HEADS4 + 1):
                    if u < HEADS4:
                        if u >= 2:
                            pe.wait_ge(ret_weights, HEADS4 * l + u - 1)
                        rows, blk = slice(64 * (u % 2), 64 * (u % 2) + 64), 6 + u // 2
                        pe.matmul(bank[u % 2][:, 0:SEQ], kT[rows, blk, 0:P], qT[rows, blk, :], start=True, stop=True)
                        pe.matmul(bank[u % 2][:, SEQ:SEQ + P], kT[rows, blk, tok(1)], qT[rows, blk, tok(1)],
                                  start=True, stop=True).then_inc(ret_scores, 1)
                    if u >= 1:
                        w = u - 1
                        pe.wait_ge(ret_weights, HEADS4 * l + w + 1)
                        src = (probs, probsT)[w // 2][:, w % 2, :]
                        val = v[:, :, 768 + 64 * w:832 + 64 * w]
                        pe.matmul(bank[5][:, w * P:w * P + 64], src[:, 0:P], val[:, 0, :], start=True, stop=True)
                        pe.matmul(bank[5][:, w * P + 64:w * P + P], src[:, P:SEQ], val[:, 0, :],
                                  start=True, stop=False)
                        pe.matmul(bank[5][:, w * P + 64:w * P + P], src[:, SEQ:3 * P], val[:, 1, :],
                                  start=False, stop=True).then_inc(ret_pv, 1)

            def accumulate(key, l):
                pe.wait_ge(out_taken, out_use[key, l])
                pieces = pieces_of[key, l]
                for c, piece in enumerate(pieces):
                    ready(piece)
                    w = parts(piece)
                    for k in range(2):
                        kk = 2 * c + k
                        rows = (xT_hi, xT_lo) if kk < KB else (yT_hi, yT_lo)
                        for t in range(NT):
                            for j in range(2):
                                last = exact(bank[4 + 2 * t + j][:, :], [x[:, kk % KB, tok(t)] for x in rows],
                                             [x[:, k, j * CHUNK:(j + 1) * CHUNK] for x in w],
                                             kk == 0, kk == 2 * len(pieces) - 1)
                    last.then_inc(pieces_used, 1)

            def dense():
                emptied(pe, ("norm", ("ffn", 0), 3))
                pe.wait_ge(out_taken, out_use["ffn", 0])
                pairs = FB_DENSE // 2

                def down(j):
                    pe.wait_ge(hid_ready, j + 1)
                    piece = pieces_of["dd", j][0]
                    ready(piece)
                    w = parts(piece)
                    for f in range(2):
                        for t in range(NT):
                            for c in range(2):
                                at0 = f * SEQ + t * P
                                last = exact(bank[4 + 2 * t + c][:, :], [x[:, j % 2, at0:at0 + P] for x in (hT_hi, hT_lo)],
                                             [x[:, f, c * CHUNK:(c + 1) * CHUNK] for x in w],
                                             j == 0 and f == 0, j == pairs - 1 and f == 1)
                    last.then_inc(pieces_used, 1)

                for j in range(pairs):
                    features([("dg", j)], ("dg", j))
                    features([("du", j)], ("du", j))
                    if j >= 1:
                        down(j - 1)
                down(pairs - 1)

            def router():
                emptied(pe, ("norm", ("ffn", 1), 3))
                free_bank(pe, ("logits",))
                for t in range(NT):
                    for k in range(KB):
                        for n, x in enumerate(x_parts(k, tok(t))):
                            last = pe.matmul(bank_of(("logits",))[:, t * 8:t * 8 + 8], x.bitcast(F32), rtw[:, k, :],
                                             start=(k == 0 and n == 0), stop=(k == KB - 1 and n == 1))
                last.then_inc(unit_full, 1)
                pe.wait_ge(members_ready, 1)
                pe.wait_ge(route_in, 16)
                free_bank(pe, ("rank",))
                b = bank_of(("rank",))
                pe.matmul(b[:, 0:8], route[:, 0, :], routing[:, 4, 0, :], start=True, stop=True)
                pe.matmul(b[:, 8:16], route[:, 0, :], routing[:, 4, 1, :], start=True, stop=False)
                pe.matmul(b[:, 8:16], route[:, 1, :], routing[:, 4, 0, :], start=False, stop=True).then_inc(unit_full, 1)
                free_bank(pe, ("rank_max",))
                pe.wait_ge(rank_max, 1)
                pe.transpose(bank_of(("rank_max",))[0:1, 0:P], lone[:, 0:1], ident[:, :]).then_inc(unit_full, 1)

            def expert(e, s, first, is_first, is_last):
                def turn_bank(x):
                    pe.wait_ge(s["tfree"], 14 * e + x - 3)
                    return bank[6 + x % 2]

                def product(what, j):
                    for half in range(2):
                        k = EXPERT_ORDER.index((what, j, half))
                        pe.wait_ge(s["low"], first + PER_EXPERT * e + k + 1)
                        if what == "down" and half == 0:
                            if j == 0 and not is_first:
                                pe.wait_ge(s["y"], e)
                            pe.wait_ge(s["tfree"], 14 * e + hidden_at(j, is_last) - 1)
                        if what == "down":
                            w = [x[:, k % PARTS, :].rearrange("p (k n) -> p k n", k=2) for x in (high, low)]
                            for f in range(2):
                                ff = 2 * half + f
                                for c in range(2):
                                    last = exact(bank[4 + c][:, :], [x[:, j % 2, ff * P:(ff + 1) * P] for x in (hT_hi, hT_lo)],
                                                 [x[:, f, c * CHUNK:(c + 1) * CHUNK] for x in w],
                                                 j == 0 and ff == 0, j == GROUPS - 1 and ff == 3)
                        else:
                            w = [x[:, k % PARTS, :].rearrange("p (k n) -> p k n", k=4) for x in (high, low)]
                            dst = bank[(0 if what == "gate" else 2) + j % 2]
                            for i in range(4):
                                kk = 4 * half + i
                                last = exact(dst[:, :], [x[:, kk, :] for x in (xg_hi, xg_lo)], [x[:, i, :] for x in w],
                                             kk == 0, kk == KB - 1)
                        last.then_inc(s["used"], 1)
                        if what == "down" and j == GROUPS - 2 and half == 0:
                            turn_hidden(GROUPS - 1)

                def turn_hidden(j):
                    b = turn_bank(hidden_at(j, is_last))
                    pe.wait_ge(s["hm"], GROUPS * e + j + 1)
                    for f in range(4):
                        last = pe.transpose(b[:, f * P:(f + 1) * P], hm[:, j % 2, f * P:(f + 1) * P], ident[:, :])
                    last.then_inc(s["tfull"], 1)

                for j in range(GROUPS):
                    if j == 0:
                        if is_first:
                            pe.wait_ge(s["tfree"], 2)
                        else:
                            pe.wait_ge(s["tfree"], 14 * e - 3)
                            pe.wait_ge(s["hm"], GROUPS * e)
                    if j >= 2:
                        pe.wait_ge(s["hm"], GROUPS * e + j - 1)
                    product("gate", j)
                    if j == 0:
                        if not is_first:
                            scatter(e, s, 0, turn_bank)
                        b = turn_bank(4)
                        for t in range(NT):
                            last = pe.transpose(b[:, t * P:(t + 1) * P], pickG[:, t, :], ident[:, :])
                        last.then_inc(s["tfull"], 1)
                    if j >= 1:
                        turn_hidden(j - 1)
                    product("up", j)
                    if j == GROUPS - 1 and not is_last:
                        gather(e + 1, s, lambda a: turn_bank(11 + a))
                    if j >= 1:
                        product("down", j - 1)
                product("down", GROUPS - 1)
                if is_last:
                    scatter(e + 1, s, 12, turn_bank)

            def gather(e, s, bank_for):
                pe.wait_ge(s["sel"], e + 1)
                for a in range(2):
                    b = bank_for(a)
                    for k in range(4):
                        for t in range(NT):
                            last = pe.matmul(b[:, k * P:(k + 1) * P], xn[:, t, (4 * a + k) * P:(4 * a + k + 1) * P],
                                             pickP[:, t, :], start=(t == 0), stop=(t == NT - 1))
                    last.then_inc(s["tfull"], 1)

            def scatter(e, s, x, turn_bank):
                pe.wait_ge(s["y"], e)
                for t in range(NT):
                    for c in range(2):
                        b = turn_bank(x + 2 * t + c)
                        pe.matmul(b[:, :], pickGT[:, 0, tok(t)], yx[:, c * CHUNK:(c + 1) * CHUNK],
                                  start=True, stop=True).then_inc(s["tfull"], 1)

            def all_experts(s, first):
                gather(0, s, lambda a: bank[6 + a])
                expert(0, s, first, True, False)
                with pe.Fori(1, N_EXPERTS - 1) as e:
                    expert(e, s, first, False, False)
                expert(N_EXPERTS - 1, s, first, False, True)

            def experts():
                router()
                for name in ("logits", "rank", "rank_max"):
                    emptied(pe, (name,))
                pe.wait_ge(out_taken, out_use["wo", 1] + 1)
                all_experts(moe_sems[0], moe_first)
                pe.wait_ge(route_ready, 1)
                over = pe.value_load(flag_i[0:1, 0:1], min_val=0, max_val=1)
                with pe.If(over > 0):
                    pe.wait_ge(moe_sems[0]["tfree"], 14 * N_EXPERTS)
                    pe.nop().then_inc(moe_sems[1]["used"], RAW)
                    all_experts(moe_sems[1], RAW)

            def layer_embedding(l):
                norm(("ple", l))
                pe.wait_ge(p_in, 16 * (l + 1))
                key = ("pT", l)
                free_bank(pe, key)
                for k in range(2):
                    for t in range(NT):
                        last = pe.transpose(bank_of(key)[:, (k * NT + t) * P:(k * NT + t + 1) * P],
                                            pin[:, t, k * P:(k + 1) * P], ident[:, :])
                last.then_inc(unit_full, 1)
                emptied(pe, key)
                piece = pieces_of["pp", l][0]
                ready(piece)
                w = parts(piece)
                for j in range(2):
                    for t in range(NT):
                        key = ("pproj", l, j, t)
                        free_bank(pe, key)
                        for k in range(2):
                            last = exact(bank_of(key)[:, :], (pT_hi[:, k, tok(t)], pT_lo[:, k, tok(t)]),
                                         [x[:, k, j * CHUNK:(j + 1) * CHUNK] for x in w], k == 0, k == 1)
                        last.then_inc(unit_full if (j, t) != (1, 1) else pieces_used, 1)
                for j in range(2):
                    rows_units([("gate", l, j, t) for t in range(NT)], ("pg", l, j))

            def hgrn(l):
                emptied(pe, ("ih", l, 1))
                pe.wait_ge(out_taken, out_use["hgrn", l])
                n = (LEVELS + 2) * l

                def heads(dst, s, t):
                    for hd in range(HEADS4):
                        last = pe.matmul(dst[:, hd * P:(hd + 1) * P], kT[:, hd, tok(s)], qT[:, hd, tok(t)],
                                         start=True, stop=True)
                    return last

                for lv in range(LEVELS + 1):
                    pe.wait_ge(hg_qk, n + lv + 1)
                    if lv >= 2:
                        pe.wait_ge(hg_placed, n + lv - 1)
                    for c in range(NT):
                        last = heads(bank[4 + 2 * (lv % 2) + c], c, c)
                    last.then_inc(hg_scores, 1)
                pe.wait_ge(hg_qk, n + LEVELS + 2)
                pe.wait_ge(hg_placed, n + LEVELS)
                heads(bank[4 + 2 * ((LEVELS + 1) % 2)], 0, 1).then_inc(hg_scores, 1)
                pe.wait_ge(hg_placed, n + LEVELS + 2)
                for t in range(NT):
                    for hd in range(HEADS4):
                        dst = bank[4 + t][:, hd * P:(hd + 1) * P]
                        last = pe.matmul(dst, atH[:, t, hd, :], v[:, t, hd * P:(hd + 1) * P],
                                         start=True, stop=(t == 0))
                        if t == 1:
                            last = pe.matmul(dst, atH[:, 2, hd, :], v[:, 0, hd * P:(hd + 1) * P],
                                             start=False, stop=True)
                last.then_inc(hg_pv, 1)

            pe.wait_ge(first_in, FIRST)
            for l in range(LAYERS):
                norm(("mix", l))
                emptied(pe, ("norm", ("mix", l), 3))
                for name in ("qa", "ka", "va", "qkb", "vfb", "qkc", "vgc"):
                    keys = [(name, l, i) for i in range(2)]
                    (features if name in ("qa", "ka", "qkb") else rows_units)(keys, (name, l))
                emptied(pe, ("vfb", l, 1))
                key = ("forgetT", l)
                free_bank(pe, key)
                for t in range(NT):
                    last = pe.transpose(bank_of(key)[0:HEADS4, tok(t)], forget_rows[:, t, :], ident[:, :])
                last.then_inc(unit_full, 1)
                pe.wait_ge(rotated, l + 1)
                for n, key in enumerate((("qcT", l), ("kcT", l))):
                    free_bank(pe, key)
                    for k in range(2):
                        for t in range(NT):
                            c0 = t * G + (2 * n + k) * P
                            last = pe.transpose(bank_of(key)[:, (k * NT + t) * P:(k * NT + t + 1) * P],
                                                a2[:, c0:c0 + P], ident[:, :])
                    last.then_inc(unit_full, 1)
                emptied(pe, ("qcT", l))
                emptied(pe, ("kcT", l))
                attention("diff", l, [("vgc", l, 1), ("qkc", l, 1)])
                attention("fox", l, [])
                retention(l)
                pe.wait_ge(y_ready, l + 1)
                turn_rows(("yT", l), y1, 4)
                emptied(pe, ("yT", l, 3))
                accumulate("wo", l)
                norm(("ffn", l))
                if l == 0:
                    dense()
                else:
                    experts()
                layer_embedding(l)
            for l in range(LAYERS):
                norm(("mem", l))
                emptied(pe, ("norm", ("mem", l), 3))
                for name in ("km", "vm"):
                    rows_units([(name, l, i) for i in range(NT)], (name, l))
                pe.wait_ge(normed, 4 * l + 1)
                turn_rows(("kmT", l), a2[:, :].rearrange("p (t d) -> p t d", t=NT), 2)
                norm(("mix2", l))
                emptied(pe, ("norm", ("mix2", l), 3))
                for name in ("qm", "qa2", "ka2", "va2"):
                    rows_units([(name, l, i) for i in range(NT)], (name, l))
                    if name == "qm":
                        pe.wait_ge(normed, 4 * l + 2)
                        turn_rows(("qmT", l), a1[:, :].rearrange("p (t d) -> p t d", t=NT), 2)
                pe.wait_ge(normed, 4 * l + 3)
                turn_rows(("qaT2", l), a1[:, :].rearrange("p (t d) -> p t d", t=NT), 2)
                pe.wait_ge(normed, 4 * l + 4)
                turn_rows(("kaT2", l), a2[:, :].rearrange("p (t d) -> p t d", t=NT), 2)
                emptied(pe, ("kaT2", l, 1))
                attention("moba", l, [("va2", l, 1)])
                attention("memory", l, [])
                for name in ("qh", "fh", "ih"):
                    (rows_units if name == "ih" else features)([(name, l, i) for i in range(2)], (name, l))
                hgrn(l)
                for c in range(3):
                    rows_units([("z", l, c, t) for t in range(NT)], ("z", l, c))
                pe.wait_ge(y_ready, LAYERS + l + 1)
                turn_rows(("yT2", l), y2, 6)
                emptied(pe, ("yT2", l, 5))
                accumulate("wo2", l)

        @block.scalar
        def _(act):
            served, split_no, high_no = [0], [0], [0]

            def split(piece):
                k, n = piece_size[piece]
                slot = part_slot[piece]
                act.wait_ge(landed[raw_slot[piece]], 16 * landings[piece])
                if piece >= PARTS:
                    act.wait_ge(pieces_used, piece - PARTS + 1)
                act.activation(high[:, slot, 0:k * n], raw[:, raw_slot[piece], 0:k * n], ACT.Copy).then_inc(high_done, 1)

            def splits(done):
                while split_no[0] <= done + PARTS and split_no[0] != moe_first and split_no[0] < len(raw_slot):
                    split(split_no[0])
                    split_no[0] += 1

            def high_rows_of(key, dst, scales=None):
                filled(act, key)
                for k in range(2):
                    last = act.activation(dst[k], bank_of(key)[:, k * SEQ:(k + 1) * SEQ], ACT.Copy,
                                          scale=1.0 if scales is None else scales[k])
                last.then_inc(high_rows, 1)

            def serve(dst, src, func, scale=1.0, bias=0.0):
                served[0] += 1
                act.wait_ge(dve_asks, served[0])
                act.activation(dst, src, func, scale=scale, bias=bias).then_inc(act_answers, 1)

            def serve_sqrt(n):
                serve(stat[:, 1, 0:n], stat[:, 0, 0:n], ACT.Sqrt)

            def norm(name):
                src = norm_input(act, name)
                if norm_no[name]:
                    act.wait_ge(xn_ready, norm_no[name])
                for t in range(NT):
                    last = act.activation(xn[:, t, :], src[:, t, :], ACT.Square, accum_out=ssum[:, t:t + 1])
                last.then_inc(squares, 1)
                serve_sqrt(NT)
                if name != "final":
                    gain = gcols[:, norm_gain[name], :]
                    for j in range(4):
                        high_rows_of(("norm", name, j), [xT_hi[:, 2 * j + k, :] for k in range(2)],
                                     [gain[:, 2 * j + k:2 * j + k + 1] for k in range(2)])

            def take(key, dst, scale=1.0, src=None, func=ACT.Copy):
                filled(act, key)
                act.activation(dst, bank_of(key)[:, :] if src is None else src, func, scale=scale).then_inc(unit_act, 1)

            def flat(tensor, c0, n):
                return tensor[:, c0:c0 + n, :].rearrange("p a b -> p (a b)")

            def attention(name, l):
                count, _, spans = att_shape(name)
                first = att_first[name, l]

                def exps(u):
                    g = first + u
                    act.wait_ge(att_max, g + 1)
                    if g >= 2:
                        act.wait_ge(att_turned, g - 1)
                    for t, (c0, n) in enumerate(spans):
                        i = u * NT + t
                        last = act.activation(probs[:, g % 2, c0:c0 + n], bank[g % 2][:, c0:c0 + n], ACT.Exp,
                                              bias=negmax[:, i:i + 1], accum_out=rowsum[:, i:i + 1])
                    last.then_inc(att_exp, 1)

                def copy(u):
                    g = first + u
                    n = spans[1][0] + spans[1][1]
                    act.wait_ge(att_turned, g + 1)
                    if g >= 2:
                        act.wait_ge(att_pv, g - 1)
                    act.activation(probsT[:, g % 2, 0:n], bank[2 + g % 2][:, 0:n], ACT.Copy).then_inc(att_copied, 1)

                for i in range(count + 1):
                    if i < count:
                        exps(i)
                    if i >= 1:
                        copy(i - 1)

            def expert_split(e, s, first, loads0, k):
                act.wait_ge(s["landed"][k % RAW], 16 * (PER_EXPERT // RAW * e + loads0[k % RAW] + k // RAW + 1))
                act.wait_ge(s["used"], first + PER_EXPERT * e + k - PARTS + 1)
                act.activation(high[:, k % PARTS, :], raw[:, k % RAW, :], ACT.Copy).then_inc(s["high"], 1)

            def gathered(s, full, banks):
                for a in range(2):
                    act.wait_ge(s["tfull"], full + a)
                    for k in range(4):
                        i = 4 * a + k
                        last = act.activation(xg_hi[:, i, :], bank[banks[a]][:, k * P:(k + 1) * P], ACT.Copy,
                                              scale=gcols[:, norm_gain["ffn", 1], i:i + 1])
                    last.then_inc(s["thigh"], 1)

            def expert(e, s, first, loads0, is_last):
                def copy(j):
                    x = hidden_at(j, is_last)
                    act.wait_ge(s["tfull"], 14 * e + x - 1)
                    act.activation(hT_hi[:, j % 2, :], bank[6 + x % 2][:, :], ACT.Copy).then_inc(s["thigh"], 1)

                for q, (what, j, half) in enumerate(EXPERT_ORDER):
                    if q + PARTS < PER_EXPERT:
                        expert_split(e, s, first, loads0, q + PARTS)
                    elif not is_last:
                        expert_split(e + 1, s, first, loads0, q + PARTS - PER_EXPERT)
                    if (what, half) == ("gate", 1):
                        if j >= 1:
                            copy(j - 1)
                        act.wait_ge(s["used"], first + PER_EXPERT * e + q + 1)
                        act.activation(gated[:, j % 2, :], bank[j % 2][:, :], ACT.Silu).then_inc(s["silu"], 1)
                    if (what, j, half) == ("up", GROUPS - 1, 1) and not is_last:
                        gathered(s, 14 * e + 10, (7, 6))
                    if (what, j, half) == ("down", GROUPS - 2, 0):
                        copy(GROUPS - 1)
                act.wait_ge(s["used"], first + PER_EXPERT * (e + 1))
                for c in range(2):
                    last = act.activation(yx[:, c * CHUNK:(c + 1) * CHUNK], bank[4 + c][:, :], ACT.Copy)
                last.then_inc(s["y"], 1)

            def all_experts(s, first, loads0):
                act.wait_ge(pieces_used, moe_first)
                for k in range(PARTS):
                    expert_split(0, s, first, loads0, k)
                gathered(s, 1, (6, 7))
                expert(0, s, first, loads0, False)
                with act.Fori(1, N_EXPERTS - 1) as e:
                    expert(e, s, first, loads0, False)
                expert(N_EXPERTS - 1, s, first, loads0, True)

            for dst, src in first_loads[:-1]:
                act.dma_start(dst, src).then_inc(first_in, 16)

            def around(key, evacuate):
                splits(pieces_of[key][0])
                evacuate()
                splits(pieces_of[key][-1])

            for l in range(LAYERS):
                norm(("mix", l))

                def mix_take(name):
                    if name == "qa":
                        for i in range(2):
                            take(("qa", l, i), flat(qT, 2 * i, 2), 0.125)
                    if name == "va":
                        for i in range(2):
                            take(("va", l, i), v[:, i, 0:512])
                    if name == "qkb":
                        take(("qkb", l, 0), flat(qT, 4, 2), 0.125)
                    if name == "vgc":
                        for i in range(2):
                            key = ("vgc", l, i)
                            filled(act, key)
                            act.activation(sg[:, i, :], bank_of(key)[:, 256:512], ACT.Silu)
                            act.activation(v[:, i, 768:1024], bank_of(key)[:, 0:256], ACT.Copy).then_inc(unit_act, 1)

                if l == 0:
                    splits(-1)
                for name in ("qa", "ka", "va", "qkb", "vfb", "qkc", "vgc"):
                    around((name, l), lambda: mix_take(name))
                    if (name, l) == ("ka", 0):
                        serve(lbs[:, 1, 1, :], lbs[:, 1, 0, :], ACT.Sigmoid)
                        serve(stat[:, 1, 0:2 * LAYERS], stat[:, 0, 0:2 * LAYERS], ACT.Exp)
                        serve(rope[:, 1, :, :], rope[:, 1, :, :], ACT.Sin)
                        serve(rope[:, 0, :, :], rope[:, 0, :, :], ACT.Sin)
                take(("qcT", l), flat(qT, 6, 2))
                take(("kcT", l), flat(kT, 6, 2))
                serve(fox[:, 1, :], fox[:, 1, :], ACT.Exp, scale=-1.0)
                serve(fox[:, 1, :], fox[:, 1, :], ACT.Ln, bias=1.0)
                attention("diff", l)
                serve_sqrt(8)
                attention("fox", l)
                serve_sqrt(8)
                for j in range(4):
                    high_rows_of(("yT", l, j), [xT_hi[:, 2 * j + k, :] for k in range(2)])
                splits(last_piece["wo", l])
                norm(("ffn", l))
                if l == 0:
                    for j in range(FB_DENSE // 2):
                        splits(pieces_of["dg", j][0])
                        filled(act, ("dg", j))
                        if j >= 2:
                            emptied(act, ("du", j - 2))
                        act.activation(gated[:, j % 2, :], bank_of(("dg", j))[:, :], ACT.Silu).then_inc(unit_act, 1)
                        splits(pieces_of["du", j][0])
                        emptied(act, ("du", j))
                        if j >= 2:
                            act.wait_ge(pieces_used, pieces_of["dd", j - 2][0] + 1)
                        act.activation(hT_hi[:, j % 2, :], hm[:, j % 2, :], ACT.Copy).then_inc(hid_high, 1)
                        if j >= 1:
                            splits(pieces_of["dd", j - 1][0])
                    splits(last_piece["ffn", 0])
                else:
                    serve(routing[:, 5, :, :], routing[:, 5, :, :], ACT.Exp)
                    act.wait_ge(route_ready, 1)
                    all_experts(moe_sems[0], moe_first, moe_landed)
                    over = act.value_load(flag_i[0:1, 0:1], min_val=0, max_val=1)
                    with act.If(over > 0):
                        act.wait_ge(pieces_used, moe_first + N_EXPERTS * PER_EXPERT)
                        act.activation(marks[:, 16:17], ident[:, 0:1], ACT.Copy).then_inc(moe_sems[1]["high"], RAW)
                        all_experts(moe_sems[1], RAW, [0] * RAW)
                        act.wait_ge(moe_sems[1]["used"], RAW + N_EXPERTS * PER_EXPERT)
                    act.wait_ge(pieces_used, moe_first + N_EXPERTS * PER_EXPERT)
                    split_no[0] = moe_first + N_EXPERTS * PER_EXPERT
                    splits(moe_first + N_EXPERTS * PER_EXPERT - 1)
                norm(("ple", l))
                key = ("pT", l)
                high_rows_of(key, [pT_hi[:, k, :] for k in range(2)])
                for j in range(2):
                    for t in range(NT):
                        take(("pproj", l, j, t), projected(j, t))
                splits(pieces_of["pp", l][0])
                for j in range(2):
                    splits(pieces_of["pg", l, j][0])
                    for t in range(NT):
                        n = (l * 2 + j) * NT + t
                        if n >= 2:
                            act.wait_ge(gate_used, n - 1)
                        take(("gate", l, j, t), gatebuf[:, n % 2, :], func=ACT.Sigmoid)
                    splits(pieces_of["pg", l, j][1])
            norm("final")
            for l in range(LAYERS):
                norm(("mem", l))
                around(("km", l), lambda: None)

                def vm_take():
                    for i in range(NT):
                        take(("vm", l, i), v[:, i, 512:1024])

                around(("vm", l), vm_take)
                serve_sqrt(2 * 4)
                for j in range(2):
                    take(("kmT", l, j), flat(kT, 4 + 2 * j, 2))
                norm(("mix2", l))
                around(("qm", l), lambda: None)
                serve_sqrt(2 * 4)
                for j in range(2):
                    take(("qmT", l, j), flat(qT, 4 + 2 * j, 2), 128.0 ** -0.5)
                around(("qa2", l), lambda: None)
                around(("ka2", l), lambda: None)
                splits(pieces_of["va2", l][0])
                for i in range(NT):
                    take(("va2", l, i), v[:, i, 0:512])
                splits(pieces_of["va2", l][1])
                serve_sqrt(2 * 8)
                for j in range(2):
                    take(("qaT2", l, j), flat(qT, 2 * j, 2), 0.125)
                serve_sqrt(2 * 8)
                for j in range(2):
                    take(("kaT2", l, j), flat(kT, 2 * j, 2))
                attention("moba", l)
                attention("memory", l)

                def gates_take(name):
                    for i in range(2):
                        key = (name, l, i)
                        if name == "qh":
                            take(key, flat(qT, 2 * i, 2), func=ACT.Silu)
                        elif name == "fh":
                            filled(act, key)
                            act.activation(a1[:, i * 512:(i + 1) * 512], bank_of(key)[:, :], ACT.Sigmoid)
                            act.activation(flat(kT, 2 * i, 2), bank_of(key)[:, :], ACT.Sigmoid,
                                           scale=-1.0).then_inc(unit_act, 1)
                        else:
                            take(key, v[:, i, 0:512])

                for name in ("qh", "fh", "ih"):
                    around((name, l), lambda: gates_take(name))
                serve_sqrt(8)
                for c in range(3):
                    splits(pieces_of["z", l, c][0])
                    for t in range(NT):
                        n = (l * 3 + c) * NT + t
                        if n >= 2:
                            act.wait_ge(z_used, n - 1)
                        take(("z", l, c, t), zbuf[:, n % 2, :], func=ACT.Silu)
                    splits(pieces_of["z", l, c][1])
                for j in range(6):
                    rows = xT_hi if j < 4 else yT_hi
                    high_rows_of(("yT2", l, j), [rows[:, (2 * j + k) % KB, :] for k in range(2)])
                splits(last_piece["wo2", l])

        @block.vector
        def _(dve):
            steps, asked, split_no, high_no = [0], [0], [0], [0]

            def split(piece):
                k, n = piece_size[piece]
                slot, src = part_slot[piece], raw[:, raw_slot[piece], 0:k * n]
                dve.wait_ge(high_done, piece + 1)
                dve.tensor_tensor(low[:, slot, 0:k * n], src, high[:, slot, 0:k * n].bitcast(F32),
                                  ALU.subtract).then_inc(low_done, 1)

            def splits(done):
                while split_no[0] <= done + PARTS and split_no[0] != moe_first and split_no[0] < len(raw_slot):
                    split(split_no[0])
                    split_no[0] += 1

            def low_rows_of(key, low_dst, high_src, scales=None):
                high_no[0] += 1
                dve.wait_ge(high_rows, high_no[0])
                for k in range(2):
                    src = bank_of(key)[:, k * SEQ:(k + 1) * SEQ]
                    if scales is None:
                        last = dve.tensor_tensor(low_dst[k], src, high_src[k].bitcast(F32), ALU.subtract)
                    else:
                        last = dve.scalar_tensor_tensor(out=low_dst[k], in0=src, scalar=scales[k],
                                                        in1=high_src[k].bitcast(F32), op0=ALU.mult, op1=ALU.subtract)
                last.then_inc(unit_dve, 1)

            mark_no = [0]

            def mark():
                mark_no[0] += 1
                return dve.tensor_copy(marks[:, mark_no[0]:mark_no[0] + 1], ident[:, 0:1])

            def link(ins):
                steps[0] += 1
                ins.then_inc(dve_step, 1)
                dve.wait_ge(dve_step, steps[0])

            def ask(ins):
                asked[0] += 1
                ins.then_inc(dve_asks, 1)
                dve.wait_ge(act_answers, asked[0])

            def rstd(sums, n, scale):
                ask(dve.tensor_scalar(stat[:, 0, 0:n], sums, scale, EPS, ALU.mult, ALU.add))
                link(dve.reciprocal(stat[:, 1, 0:n], stat[:, 1, 0:n]))

            def norm(name):
                src = norm_input(dve, name)
                dve.wait_ge(squares, norm_no[name] + 1)
                rstd(ssum[:, :], NT, 1.0 / D)
                if name == "final":
                    dve.wait_ge(final_in, 16)
                    for t in range(NT):
                        link(dve.tensor_scalar(h[:, t, :], h[:, t, :], stat[:, 1, t:t + 1], None, ALU.mult))
                        last = dve.tensor_tensor(h[:, t, :], h[:, t, :], g_final, ALU.mult)
                    last.then_inc(h_ready, 1)
                    dve.wait_ge(h_ready, h_at["final"])
                    mark().then_inc(xn_ready, 1)
                    return
                for t in range(NT):
                    last = dve.tensor_scalar(xn[:, t, :], src[:, t, :], stat[:, 1, t:t + 1], None, ALU.mult)
                last.then_inc(xn_ready, 1)
                gain = gcols[:, norm_gain[name], :]
                for j in range(4):
                    ks = range(2 * j, 2 * j + 2)
                    low_rows_of(("norm", name, j), [xT_lo[:, k, :] for k in ks], [xT_hi[:, k, :] for k in ks],
                                [gain[:, k:k + 1] for k in ks])

            def take(key, dst, src=None):
                filled(dve, key)
                dve.tensor_copy(dst, bank_of(key)[:, :] if src is None else src).then_inc(unit_dve, 1)

            def flat(tensor, c0, n):
                return tensor[:, c0:c0 + n, :].rearrange("p a b -> p (a b)")

            def add_acc(key, l):
                dve.wait_ge(pieces_used, last_piece[key, l] + 1)
                for t in range(NT):
                    for j in range(2):
                        cols = slice(j * CHUNK, (j + 1) * CHUNK)
                        last = dve.tensor_tensor(h[:, t, cols], h[:, t, cols], bank[4 + 2 * t + j][:, :], ALU.add)
                last.then_inc(out_taken, 1)
                dve.wait_ge(out_taken, out_use[key, l] + 1)
                mark().then_inc(h_ready, 1)

            def attention(name, l):
                count, _, spans = att_shape(name)
                first = att_first[name, l]
                for u in range(count):
                    g = first + u
                    b = bank[g % 2]
                    dve.wait_ge(att_scores, g + 1)
                    for t, (c0, n) in enumerate(spans):
                        i = u * NT + t
                        last = dve.tensor_reduce(negmax[:, i:i + 1], b[:, c0:c0 + n], AX_X, ALU.max, negate=True)
                    last.then_inc(att_max, 1)
                dve.wait_ge(att_pv, first + count)
                link(dve.reciprocal(rinv[:, 0:count * NT], rowsum[:, 0:count * NT]))

            def per(x, n):
                return x.unsqueeze(len(x.shape)).to_broadcast([*x.shape, n])

            def gained(rows, heads, n, gain):
                r = stat[:, 1, 0:NT * heads].rearrange("p (t h) -> p t h", t=NT)
                link(dve.tensor_tensor(rows, rows, per(r, n), ALU.mult))
                g4 = gain.unsqueeze(1).unsqueeze(1).to_broadcast([P, NT, heads, n])
                return dve.tensor_tensor(rows, rows, g4, ALU.mult)

            def head_squares(rows, heads, n):
                sq = scr[:, 0:NT * heads * n].rearrange("p (t h n) -> p t h n", t=NT, h=heads)
                link(dve.tensor_tensor(sq, rows, rows, ALU.mult))
                link(dve.tensor_reduce(rinv[:, 0:NT * heads], sq, AX_X, ALU.add))
                rstd(rinv[:, 0:NT * heads], NT * heads, 1.0 / n)

            def head_norm(buf, heads, gain):
                n = G // heads
                rows = buf[:, :].rearrange("p (t h n) -> p t h n", t=NT, h=heads)
                head_squares(rows, heads, n)
                return gained(rows, heads, n, gain)

            def rotate(x, heads, off, half, cs, dst):
                x1, x2 = x[:, :, :, off:off + half], x[:, :, :, off + half:off + 2 * half]
                cos, sin = (cs[:, n, :, :].unsqueeze(2).to_broadcast([P, NT, heads, half]) for n in range(2))
                t1 = scr[:, 0:512].rearrange("p (t h n) -> p t h n", t=NT, h=8)[:, :, 0:heads, 0:half]
                t2 = scr[:, 512:1024].rearrange("p (t h n) -> p t h n", t=NT, h=8)[:, :, 0:heads, 0:half]
                t3 = fourth.rearrange("p (t h n) -> p t h n", t=NT, h=8)[:, :, 0:heads, 0:half]
                dve.tensor_tensor(t1, x1, cos, ALU.mult)
                dve.tensor_tensor(t2, x2, sin, ALU.mult)
                link(dve.tensor_tensor(t3, x1, sin, ALU.mult))
                link(dve.tensor_tensor(dst[:, :, :, off:off + half], t1, t2, ALU.subtract))
                link(dve.tensor_tensor(t1, x2, cos, ALU.mult))
                return dve.tensor_tensor(dst[:, :, :, off + half:off + 2 * half], t3, t1, ALU.add)

            fourth = probs[:, 0, :]

            def setup():
                dve.tensor_copy(masks[:, :, :].rearrange("p n t -> p (n t)"), a2[:, :])
                qk = scr[:, 0:512].rearrange("p (n d) -> p n d", n=8)
                for n in range(2):
                    dve.tensor_tensor(scr[:, 512 + 128 * n:640 + 128 * n].rearrange("p (l d) -> p l d", l=2),
                                      qk[:, 4 * n:4 * n + 2, :], qk[:, 4 * n + 2:4 * n + 4, :], ALU.mult)
                link(mark())
                link(dve.tensor_tensor(lbs[:, 1, 0, :], lbs[:, 0, 1, :], lbs[:, 0, 0, :], ALU.subtract))
                ask(mark())
                ask(dve.tensor_reduce(stat[:, 0, 0:4], scr[:, 512:768].rearrange("p (n d) -> p n d", n=4),
                                      AX_X, ALU.add))
                link(dve.tensor_tensor(lam[:, :], stat[:, 1, 0:2], stat[:, 1, 2:4], ALU.subtract))
                for l in range(LAYERS):
                    link(dve.tensor_scalar(lam[:, l:l + 1], lam[:, l:l + 1], lam_init(l), None, ALU.add))
                    link(dve.tensor_scalar(g_subln[:, l, :], g_subln[:, l, :], 1.0 - lam_init(l), None, ALU.mult))
                link(dve.memset(lbs[:, 1, 0, :], 0.0))
                link(dve.tensor_scalar(lbs[:, 0, :, :], lbs[:, 1, :, :], -1.0, 1.0, ALU.mult, ALU.add))
                link(dve.tensor_copy(stat[:, 0, 0:NT], pos_i[:, :]))
                ang = rope[:, 1, :, :]
                turns, part = (scr[:, 16 * n:16 * n + 16].rearrange("p (t n) -> p t n", t=NT) for n in range(2))
                link(dve.tensor_tensor(ang, per(stat[:, 0, 0:NT], ROPE_HALF),
                                       inv_rope[:, :].unsqueeze(1).to_broadcast([P, NT, ROPE_HALF]), ALU.mult))
                link(dve.tensor_scalar(turns, ang, 1.0 / TWO_PI, ROUND, ALU.mult, ALU.add))
                link(dve.tensor_scalar(turns, turns, -ROUND, None, ALU.add))
                for piece in (PI_HI, PI_MID, PI_LO):
                    link(dve.tensor_scalar(part, turns, -piece, None, ALU.mult))
                    link(dve.tensor_tensor(ang, ang, part, ALU.add))
                link(dve.tensor_scalar(ang, ang, 3.1415925, -3.1415925, ALU.min, ALU.max))
                link(dve.tensor_scalar(part, ang, -1.0, None, ALU.mult))
                link(dve.tensor_tensor(part, part, ang, ALU.max))
                ask(dve.tensor_scalar(rope[:, 0, :, :], part, -1.0, math.pi / 2, ALU.mult, ALU.add))
                ask(mark())

            def around(key, evacuate):
                splits(pieces_of[key][0])
                evacuate()
                splits(pieces_of[key][-1])

            def mix_take(name, l):
                if name == "ka":
                    take(("ka", l, 0), flat(kT, 0, 2))
                    take(("ka", l, 1), flat(kT, 2, 2))
                if name == "qkb":
                    take(("qkb", l, 1), flat(kT, 4, 2))
                if name == "vfb":
                    for i in range(NT):
                        key = ("vfb", l, i)
                        filled(dve, key)
                        dve.tensor_copy(forget_rows[:, i, :], bank_of(key)[:, 256:260])
                        dve.tensor_copy(v[:, i, 512:768], bank_of(key)[:, 0:256]).then_inc(unit_dve, 1)
                if name == "qkc":
                    for i in range(NT):
                        take(("qkc", l, i), a1[:, i * G:(i + 1) * G])

            def mixer(l):
                if l == 0:
                    splits(-1)
                for name in ("qa", "ka", "va", "qkb", "vfb", "qkc", "vgc"):
                    around((name, l), lambda: mix_take(name, l))
                    if (name, l) == ("ka", 0):
                        dve.wait_ge(consts_in, CONSTS)
                        setup()
                key = ("forgetT", l)
                filled(dve, key)
                dve.tensor_scalar(fox[:, 0, :], bank_of(key)[0:HEADS4, 0:SEQ], bforget[:, l:l + 1], None,
                                  ALU.add).then_inc(unit_dve, 1)
                emptied(dve, ("qkc", l, 1))
                rotate(a1[:, :].rearrange("p (t h n) -> p t h n", t=NT, h=8), 8, 0, 32, rot,
                       a2[:, :].rearrange("p (t h n) -> p t h n", t=NT, h=8)).then_inc(rotated, 1)
                emptied(dve, key)
                link(dve.tensor_scalar(fox[:, 1, :], fox[:, 0, :], -1.0, None, ALU.mult))
                ask(dve.tensor_tensor(fox[:, 1, :], fox[:, 1, :], fox[:, 0, :], ALU.max))
                ask(dve.tensor_scalar(fox[:, 0, :], fox[:, 0, :], 0.0, None, ALU.min))
                link(dve.tensor_tensor(fox[:, 0, :], fox[:, 0, :], fox[:, 1, :], ALU.subtract))
                link(dve.memset(fox[:, 1, :], 1.0))
                link(dve.tensor_tensor_scan(fox[:, 2, :], fox[:, 1, :], fox[:, 0, :], 0.0, ALU.mult, ALU.add))
                dve.tensor_scalar(fox[:, 3, :], fox[:, 2, :], -1.0, None, ALU.mult).then_inc(cum_ready, 1)
                attention("diff", l)
                r4 = rinv[:, :].rearrange("p (h n t) -> p h n t", h=4, n=2)
                link(dve.tensor_scalar(r4[:, :, 1, :], r4[:, :, 1, :], lam[:, l:l + 1], None, ALU.mult))
                ya = y1[:, :, 0:512].rearrange("p t (h n) -> p t h n", h=4)
                second = scr[:, :].rearrange("p (t h n) -> p t h n", t=NT, h=4)
                for hd in range(4):
                    o = bank[4 + hd][:, :].rearrange("p (n t d) -> p n t d", n=2, t=NT)
                    dve.tensor_tensor(ya[:, :, hd, :], o[:, 0], per(r4[:, hd, 0, :], P), ALU.mult)
                    last = dve.tensor_tensor(second[:, :, hd, :], o[:, 1], per(r4[:, hd, 1, :], P), ALU.mult)
                last.then_inc(out_taken, 1)
                dve.wait_ge(out_taken, out_use["diff", l] + 1)
                link(dve.tensor_tensor(ya, ya, second, ALU.subtract))
                head_squares(ya, 4, P)
                link(gained(ya, 4, P, g_subln[:, l, :]))
                attention("fox", l)
                dve.tensor_tensor(y1[:, :, 512:768].rearrange("p t (h n) -> p h t n", h=4),
                                  bank[4][:, :].rearrange("p (h t n) -> p h t n", h=4, t=NT),
                                  per(rinv[:, 0:8].rearrange("p (h t) -> p h t", h=4), 64),
                                  ALU.mult).then_inc(out_taken, 1)
                for u in range(HEADS4):
                    dve.wait_ge(ret_scores, HEADS4 * l + u + 1)
                    dve.tensor_tensor((probs, probsT)[u // 2][:, u % 2, 0:3 * P], bank[u % 2][:, 0:3 * P],
                                      decay[:, u, :], ALU.mult).then_inc(ret_weights, 1)
                dve.wait_ge(ret_pv, HEADS4 * (l + 1))
                yc = y1[:, :, 768:1024].rearrange("p t (h n) -> p t h n", h=4)
                dve.tensor_copy(yc.rearrange("p t h n -> p h t n"),
                                bank[5][:, :].rearrange("p (h t n) -> p h t n", h=4, t=NT)).then_inc(out_taken, 1)
                dve.wait_ge(out_taken, out_use["ret", l] + 1)
                link(dve.tensor_reduce(rinv[:, 0:8], yc, AX_X, ALU.add))
                link(dve.tensor_scalar(rinv[:, 0:8], rinv[:, 0:8], 1.0 / 64, None, ALU.mult))
                link(dve.tensor_tensor(yc, yc, per(rinv[:, 0:8].rearrange("p (t h) -> p t h", t=NT), 64),
                                       ALU.subtract))
                head_squares(yc, 4, 64)
                r = stat[:, 1, 0:8].rearrange("p (t h) -> p t h", t=NT)
                link(dve.tensor_tensor(yc, yc, per(r, 64), ALU.mult))
                ycf = y1[:, :, 768:1024]
                link(dve.tensor_tensor(ycf, ycf, g_ret[:, l, :].unsqueeze(1).to_broadcast([P, NT, 256]), ALU.mult))
                emptied(dve, ("vgc", l, 1))
                dve.tensor_tensor(ycf, ycf, sg[:, :, :], ALU.mult).then_inc(y_ready, 1)
                for j in range(4):
                    ks = range(2 * j, 2 * j + 2)
                    low_rows_of(("yT", l, j), [xT_lo[:, k, :] for k in ks], [xT_hi[:, k, :] for k in ks])
                splits(last_piece["wo", l])
                add_acc("wo", l)

            def dense():
                for j in range(FB_DENSE // 2):
                    splits(pieces_of["dg", j][0])
                    emptied(dve, ("dg", j))
                    filled(dve, ("du", j))
                    if j >= 2:
                        dve.wait_ge(hid_ready, j - 1)
                    dve.tensor_tensor(hm[:, j % 2, :], gated[:, j % 2, :], bank_of(("du", j))[:, :],
                                      ALU.mult).then_inc(unit_dve, 1)
                    splits(pieces_of["du", j][0])
                    dve.wait_ge(hid_high, j + 1)
                    dve.tensor_tensor(hT_lo[:, j % 2, :], hm[:, j % 2, :], hT_hi[:, j % 2, :].bitcast(F32),
                                      ALU.subtract).then_inc(hid_ready, 1)
                    if j >= 1:
                        splits(pieces_of["dd", j - 1][0])
                splits(last_piece["ffn", 0])
                add_acc("ffn", 0)

            LG, TOP, GT, EQ, MEM, EX, RANK, CE, CMB, TMP = range(10)

            def routes():
                def r(n):
                    return routing[:, n, :, :]

                def wide(x):
                    return x.to_broadcast([P, NT, N_EXPERTS])

                take(("logits",), r(LG), bank_of(("logits",))[:, 0:16].rearrange("p (t n) -> p t n", t=NT))
                emptied(dve, ("logits",))
                for t in range(NT):
                    link(dve.max(routing[:, TOP, t, :], routing[:, LG, t, :]))
                first, second = wide(routing[:, TOP, :, 0:1]), wide(routing[:, TOP, :, 1:2])
                link(dve.tensor_tensor(r(GT), r(LG), second, ALU.is_gt))
                link(dve.tensor_tensor(r(EQ), r(LG), second, ALU.is_equal))
                link(dve.memset(r(TMP), 1.0))
                for t in range(NT):
                    link(dve.tensor_tensor_scan(routing[:, CE, t, :], routing[:, TMP, t, :], routing[:, EQ, t, :],
                                                0.0, ALU.mult, ALU.add))
                link(dve.tensor_reduce(rinv[:, 0:NT], r(GT), AX_X, ALU.add))
                link(dve.tensor_tensor(r(CE), r(CE), per(rinv[:, 0:NT], N_EXPERTS), ALU.add))
                link(dve.tensor_scalar(r(CE), r(CE), 2.0, None, ALU.is_le))
                link(dve.tensor_tensor(r(EQ), r(EQ), r(CE), ALU.mult))
                dve.tensor_tensor(r(MEM), r(GT), r(EQ), ALU.add).then_inc(members_ready, 1)
                ask(dve.tensor_tensor(r(EX), r(LG), first, ALU.subtract))
                dve.wait_ge(members_ready, 1)
                link(dve.tensor_tensor(r(EX), r(EX), r(MEM), ALU.mult))
                link(dve.tensor_reduce(rinv[:, 0:NT], r(EX), AX_X, ALU.add))
                link(dve.reciprocal(rinv[:, 2:2 + NT], rinv[:, 0:NT]))
                link(dve.tensor_tensor(r(CMB), r(EX), per(rinv[:, 2:2 + NT], N_EXPERTS), ALU.mult))
                key = ("rank",)
                filled(dve, key)
                dve.tensor_scalar(r(RANK), bank_of(key)[:, 0:16].rearrange("p (t n) -> p t n", t=NT), 1.0, None,
                                  ALU.add).then_inc(unit_dve, 1)
                emptied(dve, key)
                link(dve.tensor_tensor(r(RANK), r(RANK), r(MEM), ALU.mult))
                link(dve.tensor_scalar(r(RANK), r(RANK), -1.0, None, ALU.add))
                dve.tensor_reduce(lone[:, 0:1], routing[:, RANK, :, :].rearrange("p t n -> p (t n)"), AX_X,
                                  ALU.max).then_inc(rank_max, 1)
                key = ("rank_max",)
                filled(dve, key)
                dve.tensor_reduce(lone[0:1, 6:7], bank_of(key)[0:1, 0:P], AX_X, ALU.max).then_inc(unit_dve, 1)
                emptied(dve, key)
                link(dve.tensor_scalar(lone[0:1, 7:8], lone[0:1, 6:7], P - 0.5, None, ALU.is_ge))
                dve.tensor_copy(flag_i[0:1, 0:1], lone[0:1, 7:8]).then_inc(route_ready, 1)

            def select(e, s, first_slot, n):
                def step(i, ins):
                    ins.then_inc(s["step"], 1)
                    dve.wait_ge(s["step"], 3 * n + i)

                one = bass.ds(e, 1)
                step(1, dve.tensor_copy(pick_place, routing[:, RANK, :, one].rearrange("p t n -> p (t n)")))
                step(2, dve.tensor_copy(pick_gate, routing[:, CMB, :, one].rearrange("p t n -> p (t n)")))
                step(3, dve.tensor_scalar(pick_place, pick_place, -float(first_slot), None, ALU.add))
                for t in range(NT):
                    dve.tensor_scalar(pickP[:, t, :], route[:, 2, :], pick_place[:, t:t + 1], None, ALU.is_equal)
                    last = dve.tensor_scalar(pickG[:, t, :], route[:, 2, :], pick_place[:, t:t + 1],
                                             pick_gate[:, t:t + 1], ALU.is_equal, ALU.mult)
                last.then_inc(s["sel"], 1)

            def gathered(s, high0, banks):
                for a in range(2):
                    dve.wait_ge(s["thigh"], high0 + a + 1)
                    for k in range(4):
                        i = 4 * a + k
                        last = dve.scalar_tensor_tensor(
                            out=xg_lo[:, i, :], in0=bank[banks[a]][:, k * P:(k + 1) * P],
                            scalar=gcols[:, norm_gain["ffn", 1], i:i + 1], in1=xg_hi[:, i, :].bitcast(F32),
                            op0=ALU.mult, op1=ALU.subtract)
                    last.then_inc(s["tfree"], 1)

            def scattered(s, e, x):
                for n in range(4):
                    t, c = n // 2, n % 2
                    cols = slice(c * CHUNK, (c + 1) * CHUNK)
                    dve.wait_ge(s["tfull"], 14 * e + x + n - 1)
                    dve.tensor_tensor(h[:, t, cols], h[:, t, cols], bank[6 + (x + n) % 2][:, :],
                                      ALU.add).then_inc(s["tfree"], 1)

            def expert_split(e, s, first, k):
                dve.wait_ge(s["high"], first + PER_EXPERT * e + k + 1)
                dve.tensor_tensor(low[:, k % PARTS, :], raw[:, k % RAW, :], high[:, k % PARTS, :].bitcast(F32),
                                  ALU.subtract).then_inc(s["low"], 1)

            def expert(e, s, first, first_slot, is_first, is_last):
                def low_hidden(j):
                    x = hidden_at(j, is_last)
                    n = 9 * e + (2 + j if j < 6 else (8 if is_last else 10))
                    dve.wait_ge(s["thigh"], n + 1)
                    dve.tensor_tensor(hT_lo[:, j % 2, :], bank[6 + x % 2][:, :], hT_hi[:, j % 2, :].bitcast(F32),
                                      ALU.subtract).then_inc(s["tfree"], 1)

                for q, (what, j, half) in enumerate(EXPERT_ORDER):
                    if q + PARTS < PER_EXPERT:
                        expert_split(e, s, first, q + PARTS)
                    elif not is_last:
                        expert_split(e + 1, s, first, q + PARTS - PER_EXPERT)
                    if (what, half) == ("gate", 1):
                        if j == 0:
                            if not is_first:
                                scattered(s, e, 0)
                            dve.wait_ge(s["tfull"], 14 * e + 3)
                            dve.tensor_copy(pickGT[:, 0, :], bank[6][:, 0:SEQ]).then_inc(s["tfree"], 1)
                        if j >= 1:
                            low_hidden(j - 1)
                    if (what, half) == ("up", 1):
                        dve.wait_ge(s["silu"], GROUPS * e + j + 1)
                        dve.wait_ge(s["used"], first + PER_EXPERT * e + q + 1)
                        dve.tensor_tensor(hm[:, j % 2, :], gated[:, j % 2, :], bank[2 + j % 2][:, :],
                                          ALU.mult).then_inc(s["hm"], 1)
                    if (what, j, half) == ("up", 2, 1) and not is_last:
                        select(e + 1, s, first_slot, e + 1)
                    if (what, j, half) == ("up", GROUPS - 1, 1) and not is_last:
                        gathered(s, 9 * e + 8, (7, 6))
                    if (what, j, half) == ("down", GROUPS - 2, 0):
                        low_hidden(GROUPS - 1)
                if is_last:
                    scattered(s, e, 12)

            def all_experts(s, first, first_slot):
                select(0, s, first_slot, 0)
                for k in range(PARTS):
                    expert_split(0, s, first, k)
                gathered(s, 0, (6, 7))
                expert(0, s, first, first_slot, True, False)
                with dve.Fori(1, N_EXPERTS - 1) as e:
                    expert(e, s, first, first_slot, False, False)
                expert(N_EXPERTS - 1, s, first, first_slot, False, True)

            pick_place, pick_gate = ssum[:, :], rinv[:, 8:8 + NT]

            def experts():
                routes()
                all_experts(moe_sems[0], moe_first, 0)
                dve.wait_ge(route_ready, 1)
                over = dve.value_load(flag_i[0:1, 0:1], min_val=0, max_val=1)
                with dve.If(over > 0):
                    for i in range(RAW):
                        dve.tensor_copy(marks[:, 24 + i:25 + i], ident[:, 0:1]).then_inc(moe_sems[1]["low"], 1)
                    all_experts(moe_sems[1], RAW, P)
                split_no[0] = moe_first + N_EXPERTS * PER_EXPERT
                splits(moe_first + N_EXPERTS * PER_EXPERT - 1)
                dve.wait_ge(moe_sems[0]["tfree"], 14 * N_EXPERTS)
                mark().then_inc(h_ready, 1)

            def layer_embedding(l):
                norm(("ple", l))
                key = ("pT", l)
                low_rows_of(key, [pT_lo[:, k, :] for k in range(2)], [pT_hi[:, k, :] for k in range(2)])
                splits(pieces_of["pp", l][0])
                for j in range(2):
                    splits(pieces_of["pg", l, j][0])
                    for t in range(NT):
                        n = (l * 2 + j) * NT + t
                        cols = slice(j * CHUNK, (j + 1) * CHUNK)
                        emptied(dve, ("gate", l, j, t))
                        product = scr[:, (n % 2) * CHUNK:(n % 2 + 1) * CHUNK]
                        if n >= 2:
                            dve.wait_ge(gate_used, n - 1)
                        link(dve.tensor_tensor(product, gatebuf[:, n % 2, :], projected(j, t), ALU.mult))
                        dve.tensor_tensor(h[:, t, cols], h[:, t, cols], product, ALU.add).then_inc(gate_used, 1)
                    splits(pieces_of["pg", l, j][1])
                dve.wait_ge(gate_used, 4 * (l + 1))
                mark().then_inc(h_ready, 1)

            def hgrn(l):
                tot = a1[:, :].rearrange("p (h s) -> p h s", h=HEADS4)
                for name in ("qh", "fh", "ih"):
                    around((name, l), lambda: None)
                for i in range(2):
                    emptied(dve, ("fh", l, i))
                for hd in range(HEADS4):
                    dve.tensor_scalar(tot[:, hd, :], tot[:, hd, :], lbs[:, 0, l, hd:hd + 1], lbs[:, 1, l, hd:hd + 1],
                                      ALU.mult, ALU.add)
                    last = dve.tensor_scalar(kT[:, hd, :], kT[:, hd, :], lbs[:, 0, l, hd:hd + 1], None, ALU.mult)
                link(last)
                link(dve.memset(at[:, :], 0.0))
                n = (LEVELS + 2) * l
                qs = qT[:, 0:HEADS4, :].rearrange("p h s -> p (h s)")
                ks = kT[:, 0:HEADS4, :].rearrange("p h s -> p (h s)")
                mark().then_inc(hg_qk, 1)

                def place(lv):
                    m = masks[:, lv, :].unsqueeze(1).to_broadcast([P, HEADS4, P])
                    for c in range(NT):
                        last = dve.copy_predicated(atH[:, c, :, :], m,
                                                   bank[4 + 2 * (lv % 2) + c][:, :].rearrange("p (h t) -> p h t", h=4))
                    last.then_inc(hg_placed, 1)
                    dve.wait_ge(hg_placed, n + lv + 1)

                for lv in range(LEVELS + 1):
                    dve.wait_ge(hg_scores, n + lv + 1)
                    if lv == 0:
                        dve.tensor_tensor(qs, qs, a1[:, :], ALU.mult).then_inc(hg_qk, 1)
                    else:
                        b = 1 << (lv - 1)
                        q4, k4, t4 = (x.rearrange("p (m two b) -> p m two b", two=2, b=b) for x in (qs, ks, a1[:, :]))
                        m = NT * G // (2 * b)
                        dve.tensor_tensor(q4[:, :, 1, :], q4[:, :, 1, :], per(t4[:, :, 0, 0], b), ALU.mult)
                        link(dve.tensor_tensor(k4[:, :, 0, :], k4[:, :, 0, :], per(t4[:, :, 1, 0], b), ALU.mult))
                        dve.tensor_tensor(t4[:, :, 0, 0], t4[:, :, 0, 0], t4[:, :, 1, 0], ALU.mult).then_inc(hg_qk, 1)
                    dve.wait_ge(hg_qk, n + lv + 2)
                    place(lv)
                dve.wait_ge(hg_scores, n + LEVELS + 2)
                dve.tensor_copy(atH[:, 2, :, :], bank[4 + 2 * ((LEVELS + 1) % 2)][:, :].rearrange(
                    "p (h t) -> p h t", h=4)).then_inc(hg_placed, 1)
                dve.wait_ge(hg_pv, l + 1)
                yh = y2[:, :, 512:1024].rearrange("p t (h n) -> p t h n", h=4)
                for t in range(NT):
                    last = dve.tensor_copy(y2[:, t, 512:1024], bank[4 + t][:, :])
                last.then_inc(out_taken, 1)
                dve.wait_ge(out_taken, out_use["hgrn", l] + 1)
                head_squares(yh, 4, P)
                link(gained(yh, 4, P, g_hgrn[:, l, :]))

            dve.wait_ge(first_in, FIRST)
            link(dve.memset(lone[:, :], 0.0))
            for l in range(LAYERS):
                norm(("mix", l))
                mixer(l)
                norm(("ffn", l))
                if l == 0:
                    dense()
                else:
                    experts()
                layer_embedding(l)
            norm("final")
            def take_rows(name, l, buf):
                for i in range(NT):
                    take((name, l, i), buf[:, i * G:(i + 1) * G])

            for l in range(LAYERS):
                norm(("mem", l))
                around(("km", l), lambda: take_rows("km", l, a2))
                around(("vm", l), lambda: None)
                emptied(dve, ("km", l, 1))
                head_norm(a2, 4, g_mem[:, 1, l, :]).then_inc(normed, 1)
                norm(("mix2", l))
                around(("qm", l), lambda: take_rows("qm", l, a1))
                emptied(dve, ("qm", l, 1))
                head_norm(a1, 4, g_mem[:, 0, l, :]).then_inc(normed, 1)

                def moba_rows(n, buf):
                    link(head_norm(buf, 8, g_moba[:, n, l, :]))
                    rows = buf[:, :].rearrange("p (t h n) -> p t h n", t=NT, h=8)
                    rotate(rows, 8, 0, ROPE_HALF, rope, rows).then_inc(normed, 1)

                around(("qa2", l), lambda: (emptied(dve, ("qmT", l, 1)), take_rows("qa2", l, a1)))
                around(("ka2", l), lambda: take_rows("ka2", l, a2))
                around(("va2", l), lambda: None)
                emptied(dve, ("ka2", l, 1))
                moba_rows(0, a1)
                dve.wait_ge(normed, 4 * l + 3)
                moba_rows(1, a2)
                attention("moba", l)
                for n in range(2):
                    last = dve.tensor_tensor(
                        y2[:, :, 256 * n:256 * n + 256].rearrange("p t (h n) -> p h t n", h=4),
                        bank[4 + n][:, :].rearrange("p (h t n) -> p h t n", h=4, t=NT),
                        per(rinv[:, 8 * n:8 * n + 8].rearrange("p (h t) -> p h t", h=4), 64), ALU.mult)
                last.then_inc(out_taken, 1)
                dve.wait_ge(out_taken, out_use["moba", l] + 1)
                attention("memory", l)
                for n in range(2):
                    last = dve.tensor_tensor(
                        y2[:, :, 1024 + 256 * n:1280 + 256 * n].rearrange("p t (h n) -> p h t n", h=2),
                        bank[6 + n][:, :].rearrange("p (h t n) -> p h t n", h=2, t=NT),
                        per(rinv[:, 4 * n:4 * n + 4].rearrange("p (h t) -> p h t", h=2), P), ALU.mult)
                last.then_inc(out_taken, 1)
                dve.wait_ge(out_taken, out_use["memory", l] + 1)
                hgrn(l)
                for c in range(3):
                    splits(pieces_of["z", l, c][0])
                    for t in range(NT):
                        n = (l * 3 + c) * NT + t
                        if t == 1:
                            splits(pieces_of["z", l, c][1])
                        emptied(dve, ("z", l, c, t))
                        cols = slice(c * G, (c + 1) * G)
                        last = dve.tensor_tensor(y2[:, t, cols], y2[:, t, cols], zbuf[:, n % 2, :], ALU.mult)
                        last.then_inc(z_used, 1)
                dve.wait_ge(z_used, 6 * (l + 1))
                mark().then_inc(y_ready, 1)
                for j in range(6):
                    his, los = (xT_hi, xT_lo) if j < 4 else (yT_hi, yT_lo)
                    ks = [(2 * j + k) % KB for k in range(2)]
                    low_rows_of(("yT2", l, j), [los[:, k, :] for k in ks], [his[:, k, :] for k in ks])
                splits(last_piece["wo2", l])
                add_acc("wo2", l)


def kernel(**inputs):
    import numpy as _np
    import concourse.bacc as _bacc
    from concourse import mybir as _mybir
    from concourse.bass_utils import run_bass_kernel_spmd as _run

    nc = _bacc.Bacc("TRN2", target_bir_lowering=False, num_devices=1)
    small = ("norm_mix", "norm_ffn", "ple_norm", "norm_g_2", "mem_norm_g_2", "hgrn_lb_logits_2", "b_forget", "positions_2")
    arrays = {name: _np.ascontiguousarray(a) for name, a in inputs.items() if name not in small}
    gains = _np.concatenate([inputs[name] for name in small[:5]], 0)
    arrays["l_gain_columns"] = _np.ascontiguousarray(gains.reshape(len(gains), KB, P).transpose(2, 0, 1))
    arrays["l_bound_logits"] = _np.ascontiguousarray(
        inputs["hgrn_lb_logits_2"].reshape(LAYERS, HEADS4, P).transpose(2, 0, 1))
    arrays["l_forget_bias"] = _np.ascontiguousarray(inputs["b_forget"].T)
    arrays["l_positions"] = _np.ascontiguousarray(inputs["positions_2"].reshape(NT, P).T)
    arrays.update(constants())
    io = {name: nc.dram_tensor(f"in_{name}", a.shape, _mybir.dt.from_np(a.dtype), kind="ExternalInput").ap()
          for name, a in arrays.items()}
    out = nc.dram_tensor("out_x", (1, SEQ, D), _mybir.dt.float32, kind="ExternalOutput").ap()
    program(nc, io, out)
    r = _run(nc, [{f"in_{name}": a for name, a in arrays.items()}], core_ids=[0])
    return r.results[0]["out_x"]
```
